# Optimizing a Trainium2 kernel written in Bass

```python
import math
import jax, jax.numpy as jnp
from jax import lax
import numpy as np

D_MODEL = 1024
BATCH = 1
SEQ = 512
DEPTH = 1

N_Q_HEADS = 16
N_KV_HEADS = 2
HEAD_DIM = 64
Q_GROUP = N_Q_HEADS // N_KV_HEADS
WINDOW = 128
BLOCK = 128
ATTN_W = N_Q_HEADS * HEAD_DIM
KV_W = N_KV_HEADS * HEAD_DIM
N_BUCKETS = 32
MAX_DISTANCE = 128
LRU_W = D_MODEL
LRU_BLOCKS = 8
LRU_BW = LRU_W // LRU_BLOCKS
CONV_W = 4
LRU_C = 8.0
N_EXPERTS = 16
N_GROUPS = 4
EXPERTS_PER_GROUP = N_EXPERTS // N_GROUPS
TOP_K = 2
EXPERT_FF = 512
ALPHA = (2 * DEPTH) ** 0.25
BETA = (8 * DEPTH) ** -0.25
LN_EPS = 1e-5
IN_SPLITS = (ATTN_W, KV_W, KV_W, LRU_W, LRU_W, D_MODEL, D_MODEL)
IN_W = sum(IN_SPLITS)

kernel_name = "hybrid_swa_rglru_grouped_moe_deepnorm_adaln"

def _layer_norm(x, g, b):
    xf = x.astype(jnp.float32)
    mu = xf.mean(-1, keepdims=True)
    var = jnp.square(xf - mu).mean(-1, keepdims=True)
    return ((xf - mu) * lax.rsqrt(var + LN_EPS) * g + b).astype(x.dtype)

def _t5_causal_bucket(dist):
    max_exact = N_BUCKETS // 2
    d = np.maximum(dist, 0)
    df = np.maximum(d, 1).astype(np.float32)
    large = max_exact + (np.log(df / max_exact) / math.log(MAX_DISTANCE / max_exact)
                         * (N_BUCKETS - max_exact)).astype(np.int32)
    large = np.minimum(large, N_BUCKETS - 1)
    return np.where(d < max_exact, d, large).astype(np.int32)

def _sliding_window_attention(q, k, v, rel_bias, sink):
    b, s, _ = q.shape
    nb = s // BLOCK
    q = q.reshape(b, nb, BLOCK, N_KV_HEADS, Q_GROUP, HEAD_DIM)

    def band(t):
        t = t.reshape(b, nb, BLOCK, N_KV_HEADS, HEAD_DIM)
        prev = jnp.pad(t[:, :-1], ((0, 0), (1, 0), (0, 0), (0, 0), (0, 0)))
        return jnp.concatenate([prev, t], axis=2)

    kb, vb = band(k), band(v)
    logits = jnp.einsum('bnqkgd,bnskd->bnkgqs', q, kb,
                        preferred_element_type=jnp.float32) * (HEAD_DIM ** -0.5)
    qi = np.arange(BLOCK)[:, None]
    sj = np.arange(2 * BLOCK)[None, :]
    dist = qi + BLOCK - sj
    in_window = (dist >= 0) & (dist < WINDOW)
    key_valid = (np.arange(nb)[:, None] * BLOCK - BLOCK + sj) >= 0
    mask = in_window[None] & key_valid[:, None, :]
    bias = rel_bias.astype(jnp.float32)[_t5_causal_bucket(dist)]
    bias = jnp.transpose(bias, (2, 0, 1)).reshape(N_KV_HEADS, Q_GROUP, BLOCK, 2 * BLOCK)
    logits = jnp.where(mask[None, :, None, None], logits + bias, -jnp.inf)
    sink_l = sink.astype(jnp.float32).reshape(N_KV_HEADS, Q_GROUP, 1, 1)
    m = jnp.maximum(logits.max(-1, keepdims=True), sink_l)
    p = jnp.exp(logits - m)
    probs = p / (p.sum(-1, keepdims=True) + jnp.exp(sink_l - m))
    out = jnp.einsum('bnkgqs,bnskd->bnqkgd', probs.astype(v.dtype), vb)
    return out.reshape(b, s, ATTN_W)

def _rg_lru(xb, conv_w, conv_b, wa, ba, wx, bx, lam):
    b, s, w = xb.shape
    xp = jnp.pad(xb, ((0, 0), (CONV_W - 1, 0), (0, 0)))
    xc = conv_b + sum(conv_w[j] * xp[:, j:j + s] for j in range(CONV_W))
    xh = xc.reshape(b, s, LRU_BLOCKS, LRU_BW)
    r = jax.nn.sigmoid(jnp.einsum('bshi,hij->bshj', xh, wa).reshape(b, s, w) + ba)
    i = jax.nn.sigmoid(jnp.einsum('bshi,hij->bshj', xh, wx).reshape(b, s, w) + bx)
    log_a = -LRU_C * r.astype(jnp.float32) * jax.nn.softplus(-lam.astype(jnp.float32))
    a = jnp.exp(log_a)
    inp = jnp.sqrt(-jnp.expm1(2.0 * log_a)) * (i * xc).astype(jnp.float32)

    def combine(lhs, rhs):
        a1, b1 = lhs
        a2, b2 = rhs
        return a1 * a2, a2 * b1 + b2

    _, h = lax.associative_scan(combine, (a, inp), axis=1)
    return h.astype(xb.dtype)

def _grouped_moe(u, router_w, router_b, w_gate, w_up, w_down):
    b, s, d = u.shape
    t = u.reshape(b * s, d)
    logits = jnp.dot(t, router_w, preferred_element_type=jnp.float32) + router_b.astype(jnp.float32)
    scores = jax.nn.softmax(logits, axis=-1)
    grouped = scores.reshape(-1, N_GROUPS, EXPERTS_PER_GROUP)
    group_score = lax.top_k(grouped, TOP_K)[0].sum(-1)
    g_sel = jnp.argmax(group_score, axis=-1)
    in_group = jnp.take_along_axis(grouped, g_sel[:, None, None], axis=1)[:, 0]
    w_top, i_top = lax.top_k(in_group, TOP_K)
    expert_idx = g_sel[:, None] * EXPERTS_PER_GROUP + i_top
    w_top = w_top / w_top.sum(-1, keepdims=True)
    combine = jnp.sum(jax.nn.one_hot(expert_idx, N_EXPERTS, dtype=jnp.float32)
                      * w_top[..., None], axis=1)
    h = jax.nn.silu(jnp.einsum('td,edf->tef', t, w_gate)) * jnp.einsum('td,edf->tef', t, w_up)
    h = h * combine[..., None].astype(h.dtype)
    out = jnp.einsum('tef,efd->td', h, w_down)
    return out.reshape(b, s, d)

def setup_inputs(seed: int = 0) -> dict:
    key = jax.random.key(seed)
    ks = jax.random.split(key, 24)

    def nrm(k, shape, scale):
        return jax.random.normal(k, shape, jnp.float32) * scale

    x = nrm(ks[0], (BATCH, SEQ, D_MODEL), 1.0)
    c = nrm(ks[1], (BATCH, D_MODEL), 1.0)
    ada_w = nrm(ks[2], (DEPTH, D_MODEL, 6 * D_MODEL), D_MODEL ** -0.5)
    ada_b = nrm(ks[3], (DEPTH, 6 * D_MODEL), 0.02)
    w_in = nrm(ks[4], (DEPTH, D_MODEL, IN_W), D_MODEL ** -0.5)
    v_lo = ATTN_W + KV_W
    w_in = w_in.at[:, :, v_lo:v_lo + KV_W].multiply(BETA)
    attn_sink = nrm(ks[5], (DEPTH, N_Q_HEADS), 0.5)
    rel_bias = nrm(ks[6], (N_BUCKETS, N_Q_HEADS), 0.5)
    conv_w = nrm(ks[7], (DEPTH, CONV_W, LRU_W), CONV_W ** -0.5)
    conv_b = nrm(ks[8], (DEPTH, LRU_W), 0.02)
    lru_wa = nrm(ks[9], (DEPTH, LRU_BLOCKS, LRU_BW, LRU_BW), LRU_BW ** -0.5)
    lru_ba = nrm(ks[10], (DEPTH, LRU_W), 0.02)
    lru_wx = nrm(ks[11], (DEPTH, LRU_BLOCKS, LRU_BW, LRU_BW), LRU_BW ** -0.5)
    lru_bx = nrm(ks[12], (DEPTH, LRU_W), 0.02)
    a_c = jax.random.uniform(ks[13], (DEPTH, LRU_W), jnp.float32, minval=0.9, maxval=0.999)
    a0 = a_c ** (1.0 / LRU_C)
    lru_lambda = jnp.log(a0) - jnp.log1p(-a0)
    w_out = nrm(ks[14], (DEPTH, D_MODEL, D_MODEL), D_MODEL ** -0.5 * BETA)
    ln1_g = 1.0 + nrm(ks[15], (DEPTH, D_MODEL), 0.02)
    ln1_b = nrm(ks[16], (DEPTH, D_MODEL), 0.02)
    router_w = nrm(ks[17], (D_MODEL, N_EXPERTS), D_MODEL ** -0.5)
    router_b = nrm(ks[18], (N_EXPERTS,), 0.01)
    moe_w_gate = nrm(ks[19], (DEPTH, N_EXPERTS, D_MODEL, EXPERT_FF), D_MODEL ** -0.5)
    moe_w_up = nrm(ks[20], (DEPTH, N_EXPERTS, D_MODEL, EXPERT_FF), D_MODEL ** -0.5)
    moe_w_down = nrm(ks[21], (DEPTH, N_EXPERTS, EXPERT_FF, D_MODEL), EXPERT_FF ** -0.5 * BETA)
    ln2_g = 1.0 + nrm(ks[22], (DEPTH, D_MODEL), 0.02)
    ln2_b = nrm(ks[23], (DEPTH, D_MODEL), 0.02)
    return {"x": x, "c": c, "ada_w": ada_w, "ada_b": ada_b, "w_in": w_in,
            "attn_sink": attn_sink, "rel_bias": rel_bias, "conv_w": conv_w, "conv_b": conv_b,
            "lru_wa": lru_wa, "lru_ba": lru_ba, "lru_wx": lru_wx, "lru_bx": lru_bx,
            "lru_lambda": lru_lambda, "w_out": w_out, "ln1_g": ln1_g, "ln1_b": ln1_b,
            "router_w": router_w, "router_b": router_b, "moe_w_gate": moe_w_gate,
            "moe_w_up": moe_w_up, "moe_w_down": moe_w_down, "ln2_g": ln2_g, "ln2_b": ln2_b}

def reference(x, c, ada_w, ada_b, w_in, attn_sink, rel_bias, conv_w, conv_b,
              lru_wa, lru_ba, lru_wx, lru_bx, lru_lambda, w_out, ln1_g, ln1_b,
              router_w, router_b, moe_w_gate, moe_w_up, moe_w_down, ln2_g, ln2_b):
    split_at = np.cumsum(IN_SPLITS)[:-1].tolist()
    c_act = jax.nn.silu(c)
    for l in range(DEPTH):
        mod = (c_act @ ada_w[l] + ada_b[l])[:, None, :]
        shift1, scale1, gate1, shift2, scale2, gate2 = jnp.split(mod, 6, axis=-1)
        u = x * (1.0 + scale1) + shift1
        q, k, v, lru_x, lru_gate, gate_a, gate_b = jnp.split(u @ w_in[l], split_at, axis=-1)
        y_a = _sliding_window_attention(q, k, v, rel_bias, attn_sink[l])
        y_b = _rg_lru(lru_x, conv_w[l], conv_b[l], lru_wa[l], lru_ba[l], lru_wx[l], lru_bx[l],
                      lru_lambda[l]) * jax.nn.gelu(lru_gate)
        y = jax.nn.sigmoid(gate_a) * y_a + jax.nn.sigmoid(gate_b) * y_b
        x = _layer_norm(ALPHA * x + gate1 * (y @ w_out[l]), ln1_g[l], ln1_b[l])
        u = x * (1.0 + scale2) + shift2
        f = _grouped_moe(u, router_w, router_b, moe_w_gate[l], moe_w_up[l], moe_w_down[l])
        x = _layer_norm(ALPHA * x + gate2 * f, ln2_g[l], ln2_b[l])
    return x


_drawn_inputs = setup_inputs


def setup_inputs(seed=0):
    import zlib

    import numpy as np

    out = dict(_drawn_inputs(seed))
    spreads = {}
    factors = {'attn_sink': 21.858,
     'lru_ba': 22.091,
     'lru_bx': 15.055,
     'ln2_g': 22.672,
     'ln2_b': 23.321,
     'router_b': 4.851,
     'rel_bias': 3.096}
    for name, (base, spread) in spreads.items():
        noise = np.random.default_rng([zlib.crc32(name.encode()), seed]).standard_normal(out[name].shape)
        drawn = base * np.exp(spread * noise) if base else spread * noise
        out[name] = __import__('jax').numpy.asarray(drawn.astype(out[name].dtype))
    for name, factor in factors.items():
        out[name] = (out[name] * factor).astype(out[name].dtype)
    return out
```

```python
import math
from contextlib import ExitStack

import numpy as np

import concourse.bass as bass
from concourse import mybir

ALU = mybir.AluOpType
ACT = mybir.ActivationFunctionType
AX = mybir.AxisListType
F32 = mybir.dt.float32
F32R = mybir.dt.float32r
I32 = mybir.dt.int32
U32 = mybir.dt.uint32

P = 128
D = 1024
KT = D // P
T = 512
NT = T // P
NQ, HD = 16, 64
WIN = 128
NBUCKET, MAXDIST = 32, 128
NE, GRP, EPG = 16, 4, 4
FF = 512
FT = FF // P
ALPHA = 2 ** 0.25
EPS = 1e-5
LRU_C = 8.0
MASKED = -1e30

COL_Q, COL_K, COL_V, COL_LX = 0, 1024, 1152, 1280
COL_LG, COL_GA, COL_GB = 2304, 3328, 4352
TILES = ([("k", 0, COL_K), ("v", 0, COL_V)]
         + [("lx", i, COL_LX + P * i) for i in range(KT)]
         + [("q", i, COL_Q + P * i) for i in range(KT)]
         + [("lg", i, COL_LG + P * i) for i in range(KT)]
         + [("gb", i, COL_GB + P * i) for i in range(KT)]
         + [("ga", i, COL_GA + P * i) for i in range(KT)])
NPROJ = len(TILES)
AT = {(kind, i): s for s, (kind, i, _) in enumerate(TILES)}
NSLOT = NPROJ + 1

NU = 16
START = [13 + (3 * n) // 2 for n in range(NU)]
UNIT_AT = {s: n for n, s in enumerate(START)}

NOVER = 7
NBLK = NE + NOVER
TCOL = NBLK + 1
CH = 12
HLR = 6

C_ID, C_LOW, C_HOT, C_TOK, C_EXP, C_LT, C_GT, C_J, C_END = 0, 128, 256, 640, 644, 660, 676, 692, 700


def constants():
    c = np.zeros((P, C_END), np.float32)
    c[:, C_ID:C_ID + P] = np.eye(P)
    c[:, C_LOW:C_LOW + P] = np.triu(np.ones((P, P)), 1)
    dist = 255 - np.arange(383)
    exact = NBUCKET // 2
    d = np.maximum(dist, 0)
    df = np.maximum(d, 1).astype(np.float32)
    large = exact + (np.log(df / exact) / math.log(MAXDIST / exact) * (NBUCKET - exact)).astype(np.int32)
    bucket = np.where(d < exact, d, np.minimum(large, NBUCKET - 1))
    for j in range(383):
        if 0 <= dist[j] < WIN:
            c[bucket[j], C_HOT + j] = 1.0
        else:
            c[NBUCKET, C_HOT + j] = MASKED
    c[NBUCKET, C_HOT + 383] = MASKED
    c[:, C_TOK:C_TOK + NT] = np.arange(P)[:, None] + P * np.arange(NT)[None]
    c[:, C_EXP:C_EXP + NE] = np.arange(NE)
    i, j = np.arange(4)[:, None], np.arange(4)[None]
    c[:, C_LT:C_LT + 16] = (i < j).astype(np.float32).ravel()
    c[:, C_GT:C_GT + 16] = (i > j).astype(np.float32).ravel()
    c[:, C_J:C_J + NOVER] = np.arange(NOVER)
    return c


def hybrid_layer(nc, x, c, ada_w, ada_b, w_in, attn_sink, rel_bias, conv_w, conv_b, lru_wa, lru_ba,
                 lru_wx, lru_bx, lru_lambda, w_out, ln1_g, ln1_b, router_w, router_b, moe_w_gate,
                 moe_w_up, moe_w_down, ln2_g, ln2_b, consts, out):
    def dram(name, shape, dt=F32):
        return nc.dram_tensor(name, shape, dt, kind="Internal").ap()

    bias_vec_d = dram("bias_vec_d", [NQ, 384])
    bias_rep_d = dram("bias_rep_d", [NQ, P, 384])
    mod_d = dram("mod_d", [32, P])
    u2_d = dram("u2_d", [T, D])
    table_d = dram("table_d", [P * TCOL, 1], I32)
    y_d = dram("y_d", [NBLK * P, D])

    ctx = ExitStack()
    with ctx:
        base = 16512
        top = [base]

        def region(nbytes):
            at = top[0]
            top[0] += nbytes
            assert top[0] <= 229344, top[0]
            return at

        def at(offset, name, shape, dt=F32):
            size = 4 * int(np.prod(shape[1:]))
            assert offset + size <= 229344, name
            return nc.alloc_sbuf_tensor_at(name, shape, dt, offset=offset), offset + size

        KB = 1024
        R_S = region(5 * KB + 768)
        R_A = region(16 * KB)
        R_B = region(16 * KB)
        R_W = region(36 * KB)
        R_Q = region(16 * KB)
        R_U = region(32 * KB)
        R_Y = region(16 * KB)
        R_Z = region(32 * KB)
        R_T = region(38 * KB)

        def small(name, shape, dt=F32):
            t, end = at(small.at, name, shape, dt)
            small.at = (end + 31) // 32 * 32
            assert small.at <= R_A
            return t
        small.at = R_S

        cst = small("cst", [P, C_END])
        ident = cst[:, C_ID:C_ID + P]
        ones = small("ones", [P, P])
        pcol = small("pcol", [P, 64])
        nba = small("nba", [P, KT])
        hbx = small("hbx", [P, KT])
        k8 = small("k8", [P, KT])
        nk8 = small("nk8", [P, KT])
        tiny = small("tiny", [P, 6, KT])
        ccol = small("ccol", [P, KT])
        cact = small("cact", [P, KT])
        mod1 = small("mod1", [P, 16])
        sinkp = small("sinkp", [P, NQ])
        mx = small("mx", [P, 4, 4])
        negm = small("negm", [P, 4, 4])
        sm = small("sm", [P, 4, 4])
        rsum = small("rsum", [P, 4, 4])
        rden = small("rden", [P, 4, 4])
        stats = small("stats", [P, 2, 6])
        aggr = small("aggr", [P, 2])
        rstd = small("rstd", [P, 1])
        epst = small("epst", [P, 1])
        wA = small("wA", [P, NT])
        wB = small("wB", [P, NT])
        yrow = small("yrow", [P, 2, NT], U32)
        ctrl = small("ctrl", [P, 9], I32)
        idn = small("idn", [P, 1], U32)

        x_sb, _ = at(R_A, "x_sb", [P, NT, D])
        xT, _ = at(R_B, "xT", [P, KT, T])
        uh, _ = at(R_U, "uh", [P, KT, T], F32R)
        ul, _ = at(R_U + 16 * KB, "ul", [P, KT, T], F32R)
        wax, _ = at(R_Q + 8 * KB, "wax", [P, 2, KT, P])
        assert R_U == R_Q + 16 * KB and R_Y == R_U + 32 * KB
        ada1, _ = at(R_Q, "ada1", [P, 8, 2 * D])
        raw = [at(R_W + 4 * KB * i, f"raw{i}", [P, 1024])[0] for i in range(3)]
        whi = [at(R_W + 12 * KB + 8 * KB * i, f"whi{i}", [P, KT, P], F32R)[0] for i in range(3)]
        wlo = [at(R_W + 16 * KB + 8 * KB * i, f"wlo{i}", [P, KT, P], F32R)[0] for i in range(3)]
        q_sb, _ = at(R_Q, "q_sb", [P, KT, T])
        yb, _ = at(R_Y, "yb", [P, KT, T])
        ix, _ = at(R_A, "ix", [P, KT, T])
        dec, _ = at(R_B, "dec", [P, KT, T])
        yh, _ = at(R_A, "yh", [P, KT, T], F32R)
        yl, _ = at(R_B, "yl", [P, KT, T], F32R)
        o = R_T
        ssb = []
        for i in range(2):
            t_, o = at(o, f"ssb{i}", [P, 2, 2, 256])
            ssb.append(t_)
        bias = []
        for i in range(2):
            t_, o = at(o, f"bias{i}", [P, 2, 2, 256])
            bias.append(t_)
        ptb, o = at(o, "ptb", [P, 2, 2, 2, P])
        onrm, o = at(o, "onrm", [P, 256])
        kk = []
        for i in range(2):
            t_, o = at(o, f"kk{i}", [P, T])
            kk.append(t_)
        vv, o = at(o, "vv", [P, NT, P])
        lru_at = o
        xpad, o = at(o, "xpad", [P, 520])
        xc = []
        for i in range(2):
            t_, o = at(o, f"xc{i}", [P, T])
            xc.append(t_)
        tt = []
        for i in range(2):
            t_, o = at(o, f"tt{i}", [P, T])
            tt.append(t_)
        assert o <= R_T + 38 * KB, o - R_T
        o = lru_at
        xg, gt = [], []
        for i in range(2):
            t_, o = at(o, f"xg{i}", [P, T])
            xg.append(t_)
            t_, o = at(o, f"gt{i}", [P, T])
            gt.append(t_)
        prm, o = at(R_T, "prm", [64, P])
        adab1, o = at(o, "adab1", [16, P])
        adab2 = small("adab2", [32, P])
        rbs, o = at(o, "rbs", [NBUCKET + 1, NQ])
        bvec, o = at(o, "bvec", [NQ, 384])
        sinkt, o = at(o, "sinkt", [P, NQ])
        ada2, _ = at(R_Z, "ada2", [P, 2, 2 * D])
        acc2, _ = at(R_Z + 16 * KB, "acc2", [P, 4 * D])
        mod2c, _ = at(R_Z, "mod2c", [P, 32])
        mod2r, _ = at(R_Z + KB, "mod2r", [32, P])
        woh, wol = [], []
        for k in range(KT):
            t_, o = at(R_Z + 8 * KB * k, f"woh{k}", [P, D], F32R)
            woh.append(t_)
            t_, _ = at(o, f"wol{k}", [P, D], F32R)
            wol.append(t_)
        rows = [at(R_W + 12 * KB + 4 * KB * i, f"row{i}", [P, D])[0] for i in range(6)]
        gate1r, g1r, b1r, a2r, b2r, zt = rows
        u2 = [at(R_W + 4 * KB * i, f"u2_{i}", [P, D])[0] for i in range(2)]
        u2T, _ = at(R_W + 8 * KB, "u2T", [P, KT, P])
        x1, _ = at(R_Q, "x1", [P, NT, D])
        def route(name, shape, dt=F32):
            t, route.at = at(route.at, name, shape, dt)
            route.at = (route.at + 31) // 32 * 32
            return t
        route.at = R_A
        rw = small("rw_sb", [P, KT, NE])
        rbr = small("rbr_sb", [1, NE])
        lg_ = route("lg_", [P, NT, NE])
        sc = route("sc", [P, NT, NE])
        cge = route("cge", [P, 256])
        cgt = route("cgt", [P, 256])
        rank = route("rank", [P, NT * GRP, EPG])
        sel = route("sel", [P, NT * GRP, EPG])
        gsc = route("gsc", [P, NT, GRP])
        grank = route("grank", [P, NT, GRP])
        r0 = route("r0", [P, NT, NE])
        r1 = route("r1", [P, NT, NE])
        mm = route("mm", [P, NT, NE])
        mpre = route("mpre", [P, NT, NE])
        mtot = route("mtot", [P, NE])
        pos = route("pos", [P, NT, NE])
        cnt = route("cnt", [P, NE])
        qq = route("qq", [P, NT, NE])
        tb = route("tb", [P, NT, NE])
        blk = route("blk", [P, NT, NE])
        ovc = route("ovc", [P, NE])
        ovi = route("ovi", [P, NE])
        ovs = route("ovs", [P, NE])
        own = route("own", [P, NOVER, NE])
        own2 = route("own2", [P, NOVER, NE])
        red = route("red", [P, 8, NT])
        ctrlf = route("ctrlf", [P, 9])
        t64 = route("t64", [P, NT, NE])
        tslot = route("tslot", [P, 2, NT], U32)
        tokid = route("tokid", [P, NT], I32)
        idx = route("idx", [P, TCOL], U32)
        mraw = [at(R_U + 4 * KB * i, f"mraw{i}", [P, 1024])[0] for i in range(CH)]
        mhi = [at(R_Z + 8 * KB * i, f"mhi{i}", [P, 2, 512], F32R)[0] for i in range(HLR)]
        mlo = [at(R_Z + 8 * KB * i + 4 * KB, f"mlo{i}", [P, 2, 512], F32R)[0] for i in range(HLR)]
        o = R_Z + 8 * KB * HLR
        xg_m, o = at(o, "xg_m", [P, D])
        xTh, o = at(o, "xTh", [P, KT, P], F32R)
        xTl, o = at(o, "xTl", [P, KT, P], F32R)
        h_sb, o = at(o, "h_sb", [P, FF])
        hTh, o = at(o, "hTh", [P, FT, P], F32R)
        hTl, o = at(o, "hTl", [P, FT, P], F32R)
        ysb, o = at(o, "ysb", [P, D])
        gate2r, _ = at(R_B, "gate2r", [P, D])
        g2r, _ = at(R_B + 4 * KB, "g2r", [P, D])
        be2r, _ = at(R_B + 8 * KB, "be2r", [P, D])
        fin = [[at(R_W + 16 * KB * i + 4 * KB * j, f"fin{i}{j}", [P, D])[0] for j in range(3)] for i in range(2)]

        psum = ctx.enter_context(nc.psum_tensor("psum", [P, 8, 512], F32))
        bank = [psum[:, i, :] for i in range(8)]
        scores = psum[:, 2:4, :].rearrange("p a (b s) -> p a b s", b=2)
        ptps = psum[:, 4:6, :].rearrange("p a (b h q) -> p a b h q", b=2, h=2)

        def sem(name):
            return ctx.enter_context(nc.semaphore(name))

        const_in, param_in, x_in, small_in = (sem(n) for n in ("const_in", "param_in", "x_in", "small_in"))
        ada1_sem = [sem(f"ada1_in{j}") for j in range(8)]
        ada2_sem = [sem(f"ada2_in{j}") for j in range(2)]
        raw_in = [sem(f"raw_in{i}") for i in range(3)]
        mraw_in = [sem(f"mraw_in{i}") for i in range(CH)]
        bias_dma, bias_in0, bias_in1, kdup_in = sem("bias_dma"), sem("bias_in0"), sem("bias_in1"), sem("kdup_in")
        bias_in = [bias_in0, bias_in1]
        lruw_in, mod2_out, rows_in, x1_in = (sem(n) for n in ("lruw_in", "mod2_out", "rows_in", "x1_in"))
        u2_st, out_st, fgather = ([sem(f"{n}{i}") for i in range(2)] for n in ("u2_st", "out_st", "fgather"))
        names = """setup_done pcol_ps bvec_ps xT_ps xT_sb mod1_ps mod1_sb u_hi u_lo split_hi split_lo proj_ps
            evac pcol_sb exp_small act_order dve_order pool_order c_done bvec_sb k_sb v_sb xpad_in conv_done
            lr_ps li_ps er_done ti_done r_done ix_done ta_done m2_done sqrt_done h_done q_sb_done
            sc_ps logit_done exp_done pt_ps pt_sb o_ps on_done ot_ps ya_done bias_used
            sq_done g_arg g_tanh gelu_done gb_tanh yb_done ga_tanh y_done y_hi y_lo
            ada2_used mod2_ps mod2_sb mod2_T mod2_row wout_ps ln_sqrt_in ln_sqrt xn_done x1_done u2_done u2T_ps u2T_sb
            logits_ps rt_exp_in rt_exp m_done pos_ps pos_done slots_done ctrl_done rows_ready
            pool_went table_z table_w idx_in gath xT_m_ps xTh_m xTl_m chunk_used mhi_done mlo_done silu_done h_done_m
            hT_ps hTh_done hTl_done y_ev0 y_ev1 y_st fin_z fin_n fin_out xn_used
            z_done idn_done pool_in t_done""".split()
        S = {n: sem(n) for n in names}

        block = ctx.enter_context(nc.Block())
        w_in_v = w_in[0].rearrange("(k p) n -> p k n", p=P)
        ada_v = ada_w[0].rearrange("(p j) n -> p j n", j=8)
        wg_v = moe_w_gate[0].rearrange("e (c k p) f -> e c p k f", p=P, k=2)
        wu_v = moe_w_up[0].rearrange("e (c k p) f -> e c p k f", p=P, k=2)
        wd_v = moe_w_down[0].rearrange("e (c p) n -> e c p n", p=P)

        def chunk_src(e, ch):
            v = (wg_v, wu_v, wd_v)[ch // 4]
            return v[e, ch % 4]

        def chunk_dst(ch):
            return mraw[ch][:, :].rearrange("p (k f) -> p k f", k=2) if ch < 8 else mraw[ch][:, :]

        @block.sync
        def _(sp):
            sp.dma_start(cst[:, :], consts).then_inc(const_in, 16)
            sp.dma_start(ccol[:, :], c[0].rearrange("(p j) -> p j", j=8)).then_inc(small_in, 16)
            sp.dma_start(adab1[:, :], ada_b[0, 0:2 * D].rearrange("(r p) -> r p", p=P)).then_inc(small_in, 16)
            for j, (a, b) in enumerate(((conv_w[0].rearrange("j (k p) -> (j k) p", p=P), 32),
                                        (conv_b[0].rearrange("(k p) -> k p", p=P), 8),
                                        (lru_ba[0].rearrange("(k p) -> k p", p=P), 8),
                                        (lru_bx[0].rearrange("(k p) -> k p", p=P), 8),
                                        (lru_lambda[0].rearrange("(k p) -> k p", p=P), 8))):
                r = (0, 32, 40, 48, 56)[j]
                sp.dma_start(prm[r:r + b, :], a).then_inc(param_in, 16)
            for t in range(NT):
                sp.dma_start(x_sb[:, t, :], x[0, t * P:(t + 1) * P, :]).then_inc(x_in, 16)
            for j in range(8):
                sp.dma_start(ada1[:, j, :], ada_v[:, j, 0:2 * D]).then_inc(ada1_sem[j], 16)

            def load_tile(t):
                if t >= 3:
                    sp.wait_ge(S["split_lo"], t - 2)
                if t < NPROJ:
                    col = TILES[t][2]
                    sp.dma_start(raw[t % 3][:, :].rearrange("p (k n) -> p k n", k=KT),
                                 w_in_v[:, :, col:col + P]).then_inc(raw_in[t % 3], 16)
                else:
                    k = t - NPROJ
                    sp.dma_start(raw[t % 3][:, :], w_out[0, k * P:(k + 1) * P, :]).then_inc(raw_in[t % 3], 16)

            for t in range(3):
                load_tile(t)
            sp.wait_ge(S["bvec_sb"], 1)
            sp.dma_start(bias_vec_d, bvec[:, :]).then_inc(bias_dma, 16)
            sp.wait_ge(bias_dma, 16)
            rep_src = bass.AP(bias_vec_d.tensor, 0, [[384, NQ], [0, P], [1, 384]])
            sp.dma_start(bias_rep_d, rep_src).then_inc(bias_dma, 16)
            sp.wait_ge(bias_dma, 32)

            def load_bias(hg):
                if hg >= 2:
                    sp.wait_ge(S["logit_done"], 4 * (hg - 1))
                for par in range(2):
                    src = bass.AP(bias_rep_d.tensor, (4 * hg + par) * P * 384 + 127,
                                  [[383, P], [2 * P * 384, 2], [1, 256]])
                    sp.dma_start(bias[hg % 2][:, par, :, :], src).then_inc(bias_in[hg % 2], 16)

            sp.wait_ge(S["mod1_ps"], 1)
            sp.dma_start(wax[:, 0, :, :], lru_wa[0].rearrange("h i j -> i h j")).then_inc(lruw_in, 16)
            sp.dma_start(wax[:, 1, :, :], lru_wx[0].rearrange("h i j -> i h j")).then_inc(lruw_in, 16)
            for t in range(3, NPROJ + KT):
                load_tile(t)
                if t == 6:
                    sp.wait_ge(S["k_sb"], 1)
                    sp.wait_ge(S["evac"], 1)
                    sp.dma_start(kk[0][64:128, :], kk[0][0:64, :]).then_inc(kdup_in, 16)
                    sp.dma_start(kk[1][0:64, :], kk[1][64:128, :]).then_inc(kdup_in, 16)
                    load_bias(0)
                    load_bias(1)
                if t == START[8] - 1:
                    load_bias(2)
                if t == START[12] - 1:
                    load_bias(3)
                if t == 36:
                    sp.wait_ge(S["mod2_row"], 1)
                    sp.dma_start(mod_d, mod2r[:, :]).then_inc(mod2_out, 16)
                    sp.wait_ge(mod2_out, 16)
            sp.wait_ge(S["proj_ps"], NPROJ)
            mod_flat = mod_d.rearrange("a b -> (a b)")

            def row_of(i):
                return mod_flat[i * D:(i + 1) * D].partition_broadcast(P)
            sp.dma_start(gate1r[:, :], row_of(0)).then_inc(rows_in, 16)
            sp.dma_start(g1r[:, :], ln1_g[0].partition_broadcast(P)).then_inc(rows_in, 16)
            sp.dma_start(b1r[:, :], ln1_b[0].partition_broadcast(P)).then_inc(rows_in, 16)
            sp.dma_start(b2r[:, :], row_of(1)).then_inc(rows_in, 16)
            sp.dma_start(a2r[:, :], row_of(2)).then_inc(rows_in, 16)
            sp.wait_ge(S["y_lo"], KT)
            for t in range(NT):
                sp.dma_start(x1[:, t, :], x[0, t * P:(t + 1) * P, :]).then_inc(x1_in, 16)
            for ch in range(CH):
                sp.dma_start(chunk_dst(ch), chunk_src(0, ch)).then_inc(mraw_in[ch], 16)
            for t in range(NT):
                sp.wait_ge(S["u2_done"], t + 1)
                sp.dma_start(u2_d[t * P:(t + 1) * P, :], u2[t % 2][:, :]).then_inc(u2_st[t % 2], 16)
            sp.wait_ge(S["wout_ps"], 2 * NT)
            sp.dma_start(gate2r[:, :], row_of(3)).then_inc(rows_in, 16)
            sp.dma_start(g2r[:, :], ln2_g[0].partition_broadcast(P)).then_inc(rows_in, 16)
            sp.dma_start(be2r[:, :], ln2_b[0].partition_broadcast(P)).then_inc(rows_in, 16)
            with sp.Fori(1, NE) as e:
                for ch in range(CH):
                    sp.wait_ge(S["mlo_done"], (e - 1) * CH + ch + 1)
                    sp.dma_start(chunk_dst(ch), chunk_src(e, ch)).then_inc(mraw_in[ch], 16)
            sp.wait_ge(S["ctrl_done"], 1)
            nblk = sp.value_load(ctrl[0:1, NOVER:NOVER + 1], min_val=NE, max_val=NBLK)
            with sp.If(nblk > NE):
                with sp.Fori(NE, nblk) as b:
                    e = sp.value_load(ctrl[0:1, bass.ds(b - NE, 1)], min_val=0, max_val=NE - 1)
                    for ch in range(CH):
                        sp.wait_ge(S["mlo_done"], (b - 1) * CH + ch + 1)
                        sp.dma_start(chunk_dst(ch), chunk_src(e, ch)).then_inc(mraw_in[ch], 16)
            for t in range(NT):
                sp.wait_ge(S["fin_out"], t + 1)
                sp.dma_start(out[0, t * P:(t + 1) * P, :], fin[t % 2][0][:, :]).then_inc(out_st[t % 2], 16)
            for q in out_st:
                sp.wait_ge(q, 16 * NT // 2)

        @block.gpsimd
        def _(pool):
            pool.dma_start(rbs[0:NBUCKET, :], rel_bias).then_inc(S["pool_in"], 16)
            pool.dma_start(sinkt[:, :], attn_sink[0].partition_broadcast(P)).then_inc(S["pool_in"], 16)
            pool.dma_start(adab2[:, :], ada_b[0, 2 * D:6 * D].rearrange("(r p) -> r p", p=P)).then_inc(S["pool_in"], 16)
            pool.dma_start(rw[:, :, :], router_w.rearrange("(k p) e -> p k e", p=P)).then_inc(S["pool_in"], 16)
            pool.dma_start(rbr[:, :], router_b.rearrange("(a e) -> a e", a=1)).then_inc(S["pool_in"], 16)
            pool.memset(acc2[:, 0:D], 0.0).then_inc(S["z_done"], 1)
            pool.wait_ge(S["z_done"], 1)
            pool.dma_start(table_d.rearrange("(p c) o -> p (c o)", p=P),
                           acc2[:, 0:TCOL].bitcast(I32)).then_inc(S["table_z"], 16)
            for b in range(NE, NBLK):
                pool.dma_start(y_d[b * P:(b + 1) * P, :], acc2[:, 0:D]).then_inc(S["table_z"], 16)
            pool.wait_ge(S["table_z"], 16 * (1 + NOVER))
            pool.wait_ge(S["c_done"], 1)
            def load_ada2(n):
                half = n % 2
                pool.dma_start(ada2[:, half, :],
                               ada_v[:, n // 2, (2 + 2 * half) * D:(4 + 2 * half) * D]).then_inc(ada2_sem[half], 16)

            load_ada2(0)
            load_ada2(1)
            for n in range(16):
                j, half = n // 2, n % 2
                part = acc2[:, half * 2 * D:(half + 1) * 2 * D]
                pool.wait_ge(ada2_sem[half], 16 * (j + 1))
                if j == 0:
                    pool.tensor_scalar(part, ada2[:, half, :], cact[:, 0:1], None, ALU.mult).then_inc(S["ada2_used"], 1)
                else:
                    pool.tensor_scalar(ada2[:, half, :], ada2[:, half, :], cact[:, j:j + 1], None,
                                       ALU.mult).then_inc(S["pool_order"], 1)
                    pool.wait_ge(S["pool_order"], n - 1)
                    pool.wait_ge(S["ada2_used"], n)
                    pool.tensor_tensor(part, part, ada2[:, half, :], ALU.add).then_inc(S["ada2_used"], 1)
                if n + 2 < 16:
                    pool.wait_ge(S["ada2_used"], n + 1)
                    load_ada2(n + 2)
            order = 14
            pool.wait_ge(rows_in, 16 * 5)
            pool.tensor_scalar(a2r[:, :], a2r[:, :], 1.0, None, ALU.add).then_inc(S["pool_order"], 1)
            pool.tensor_scalar(gate1r[:, :], gate1r[:, :], 0.5, None, ALU.mult).then_inc(S["pool_order"], 1)
            pool.wait_ge(S["pool_order"], order + 1)
            pool.tensor_tensor(zt[:, :], b1r[:, :], a2r[:, :], ALU.mult).then_inc(S["pool_order"], 1)
            pool.wait_ge(S["pool_order"], order + 3)
            pool.tensor_tensor(a2r[:, :], a2r[:, :], g1r[:, :], ALU.mult).then_inc(S["pool_order"], 1)
            pool.wait_ge(S["pool_order"], order + 4)
            pool.tensor_tensor(b2r[:, :], b2r[:, :], zt[:, :], ALU.add).then_inc(S["rows_ready"], 1)
            pool.tensor_scalar(g1r[:, :], g1r[:, :], ALPHA, None, ALU.mult).then_inc(S["pool_order"], 1)
            pool.tensor_scalar(b1r[:, :], b1r[:, :], ALPHA, None, ALU.mult).then_inc(S["pool_order"], 1)
            order += 6
            pool.wait_ge(S["pool_order"], order)
            for t in range(NT):
                pool.wait_ge(S["xn_done"], t + 1)
                pool.tensor_tensor(x1[:, t, :], zt[:, :], g1r[:, :], ALU.mult).then_inc(S["xn_used"], 1)
                pool.wait_ge(S["xn_used"], t + 1)
                pool.tensor_tensor(x1[:, t, :], x1[:, t, :], b1r[:, :], ALU.add).then_inc(S["x1_done"], 1)
            pool.wait_ge(S["slots_done"], 1)
            for t in range(NT):
                for r in range(2):
                    pool.indirect_dma_start(table_d, bass.IndirectOffsetOnAxis(ap=tslot[:, r, t:t + 1], axis=0),
                                            tokid[:, t:t + 1], None).then_inc(S["table_w"], 16)
            pool.wait_ge(S["table_w"], 16 * 2 * NT)
            pool.dma_start(idx[:, :].bitcast(I32), table_d.rearrange("(p c) o -> p (c o)", p=P)).then_inc(S["idx_in"], 16)
            pool.wait_ge(S["idx_in"], 16)
            for q in u2_st:
                pool.wait_ge(q, 16 * NT // 2)
            pool.indirect_dma_start(xg_m[:, :], None, u2_d,
                                    bass.IndirectOffsetOnAxis(ap=idx[:, 0:1], axis=0)).then_inc(S["gath"], 16)

            def block_io(b):
                pool.wait_ge(S["xT_m_ps"], b + 1)
                pool.tensor_copy(idn[:, :], idx[:, bass.ds(b + 1, 1)]).then_inc(S["idn_done"], 1)
                pool.wait_ge(S["idn_done"], b + 1)
                pool.sem_inc(S["pool_went"], 1)
                pool.indirect_dma_start(xg_m[:, :], None, u2_d,
                                        bass.IndirectOffsetOnAxis(ap=idn[:, 0:1], axis=0)).then_inc(S["gath"], 16)
                pool.wait_ge(S["y_ev0"], b + 1)
                pool.wait_ge(S["y_ev1"], b + 1)
                pool.sem_inc(S["pool_went"], 1)
                pool.dma_start(y_d[bass.ds(b * P, P), :], ysb[:, :]).then_inc(S["y_st"], 16)

            with pool.Fori(0, NE) as b:
                block_io(b)
            nblk = pool.value_load(ctrl[0:1, NOVER:NOVER + 1], min_val=NE, max_val=NBLK)
            with pool.If(nblk > NE):
                with pool.Fori(NE, nblk) as b:
                    block_io(b)
            pool.wait_ge(S["y_st"], nblk * 16)
            pool.sem_inc(S["pool_went"], 1)
            pool.wait_ge(S["x1_done"], NT)
            for t in range(NT):
                if t >= 2:
                    pool.wait_ge(S["fin_z"], t - 1)
                for r in range(2):
                    pool.indirect_dma_start(fin[t % 2][1 + r][:, :], None, y_d,
                                            bass.IndirectOffsetOnAxis(ap=yrow[:, r, t:t + 1], axis=0)).then_inc(fgather[t % 2], 16)

        @block.scalar
        def _(act):
            A = act.activation
            n_order = [0]

            def mark(ins):
                n_order[0] += 1
                ins.then_inc(S["act_order"], 1)
                return n_order[0]

            act.wait_ge(small_in, 32)
            A(tiny[:, 0, :], ccol[:, :], ACT.Exp, scale=-1.0).then_inc(S["exp_small"], 1)
            act.wait_ge(S["pcol_ps"], 1)
            A(pcol[:, :], bank[7][:, 0:64], ACT.Copy).then_inc(S["pcol_sb"], 1)
            act.wait_ge(S["bvec_ps"], 1)
            A(bvec[:, :], psum[0:16, 6, 0:384], ACT.Copy).then_inc(S["bvec_sb"], 1)
            act.wait_ge(S["dve_order"], 2)
            A(tiny[:, 1, :], tiny[:, 1, :], ACT.Exp).then_inc(S["exp_small"], 1)
            for k in range(KT):
                act.wait_ge(S["xT_ps"], k + 1)
                A(xT[:, k, :], bank[k % 4], ACT.Copy).then_inc(S["xT_sb"], 1)

            def split(t):
                act.wait_ge(raw_in[t % 3], 16 * (t // 3 + 1))
                if t < NPROJ:
                    if t >= 3:
                        act.wait_ge(S["proj_ps"], t - 2)
                        act.wait_ge(S["split_lo"], t - 2)
                    A(whi[t % 3][:, :, :], raw[t % 3][:, :].rearrange("p (k n) -> p k n", k=KT), ACT.Copy)\
                        .then_inc(S["split_hi"], 1)
                else:
                    k = t - NPROJ
                    act.wait_ge(S["mod2_row"], 1)
                    act.wait_ge(mod2_out, 16)
                    if k >= 4:
                        act.wait_ge(S["ot_ps"], NU)
                        act.wait_ge(S["y_done"], KT)
                    A(woh[k][:, :], raw[t % 3][:, :], ACT.Copy).then_inc(S["split_hi"], 1)

            split(0)
            split(1)
            for k in range(KT):
                act.wait_ge(S["mod1_sb"], k + 2)
                A(uh[:, k, :], xT[:, k, :], ACT.Copy).then_inc(S["u_hi"], 1)

            def evacuate(s):
                kind, i, _ = TILES[s]
                b = bank[s % 2]
                act.wait_ge(S["proj_ps"], s + 1)
                if kind == "k":
                    A(kk[0][0:64, :], psum[0:64, s % 2, :], ACT.Copy).then_inc(S["k_sb"], 1)
                    A(kk[1][64:128, :], psum[64:128, s % 2, :], ACT.Copy).then_inc(S["evac"], 1)
                elif kind == "v":
                    A(vv[:, :, :], b.rearrange("p (t n) -> p t n", t=NT), ACT.Copy).then_inc(S["evac"], 1)
                elif kind == "lx":
                    if i >= 1:
                        act.wait_ge(S["conv_done"], i)
                    A(xpad[:, 3:3 + T], b, ACT.Copy).then_inc(S["evac"], 1)
                elif kind == "q":
                    A(q_sb[:, i, :], b, ACT.Copy, scale=HD ** -0.5).then_inc(S["evac"], 1)
                elif kind == "lg":
                    if i >= 2:
                        act.wait_ge(S["gelu_done"], i - 1)
                    A(gt[i % 2][:, :], b, ACT.Square).then_inc(S["sq_done"], 1)
                    A(xg[i % 2][:, :], b, ACT.Copy).then_inc(S["evac"], 1)
                elif kind == "gb":
                    act.wait_ge(S["gelu_done"], min(KT, KT - 1 + i))
                    if i >= 2:
                        act.wait_ge(S["yb_done"], i - 1)
                    A(gt[i % 2][:, :], b, ACT.Tanh, scale=0.5).then_inc(S["evac"], 1)
                else:
                    act.wait_ge(S["yb_done"], min(KT, KT - 1 + i))
                    if i >= 2:
                        act.wait_ge(S["y_done"], i - 1)
                    A(gt[i % 2][:, :], b, ACT.Tanh, scale=0.5).then_inc(S["evac"], 1)

            for s in range(NPROJ + 2):
                i = s - 6
                if 0 <= i < KT:
                    act.wait_ge(S["r_done"], i + 1)
                    if i >= 2:
                        act.wait_ge(S["m2_done"], i - 1)
                    A(tt[i % 2][:, :], dec[:, i, :], ACT.Tanh, scale=k8[:, i:i + 1]).then_inc(S["t_done"], 1)
                    act.wait_ge(S["t_done"], i + 1)
                    A(dec[:, i, :], dec[:, i, :], ACT.Exp, scale=nk8[:, i:i + 1]).then_inc(S["ta_done"], 1)
                if 1 <= s <= NPROJ:
                    evacuate(s - 1)
                i = s - 5
                if 0 <= i < KT:
                    act.wait_ge(S["lr_ps"], i + 1)
                    A(dec[:, i, :], bank[6], ACT.Exp, bias=nba[:, i:i + 1], scale=-1.0).then_inc(S["er_done"], 1)
                if s + 2 < NPROJ + KT:
                    split(s + 2)
                i = s - 5
                if 0 <= i < KT:
                    act.wait_ge(S["li_ps"], i + 1)
                    A(ix[:, i, :], bank[7], ACT.Tanh, bias=hbx[:, i:i + 1], scale=0.5).then_inc(S["ti_done"], 1)
                if s == 15:
                    act.wait_ge(S["m2_done"], KT)
                    A(yb[:, :, :], yb[:, :, :], ACT.Sqrt).then_inc(S["sqrt_done"], 1)
                n = UNIT_AT.get(s - 3)
                if n is not None:
                    act.wait_ge(S["pt_ps"], n + 1)
                    if n >= 1:
                        act.wait_ge(S["o_ps"], n)
                    if n % 4 == 0:
                        A(ptb[:, :, :, 1, :], ptps[:, :, :, 1, :], ACT.Copy).then_inc(S["pt_sb"], 1)
                    else:
                        A(ptb[:, :, :, :, :], ptps[:, :, :, :, :], ACT.Copy).then_inc(S["pt_sb"], 1)
                n = UNIT_AT.get(s - 5)
                if n is not None:
                    hg, blk_ = n // 4, n % 4
                    act.wait_ge(S["ot_ps"], n + 1)
                    A(q_sb[:, 2 * hg:2 * hg + 2, blk_ * P:(blk_ + 1) * P],
                      bank[7][:, 0:256].rearrange("p (i q) -> p i q", i=2), ACT.Copy).then_inc(S["ya_done"], 1)
                i = s - (AT["lg", 0] + 1)
                if 0 <= i < KT:
                    act.wait_ge(S["g_arg"], i + 1)
                    A(gt[i % 2][:, :], gt[i % 2][:, :], ACT.Tanh, scale=math.sqrt(2 / math.pi)).then_inc(S["g_tanh"], 1)
                n = UNIT_AT.get(s - 1)
                if n is not None:
                    act.wait_ge(S["logit_done"], n + 1)
                    lo = P if n % 4 == 0 else 0
                    for a in range(2):
                        for b in range(2):
                            v = ssb[n % 2][:, a, b, lo:256]
                            A(v, v, ACT.Exp, bias=negm[:, n % 4, 2 * a + b:2 * a + b + 1],
                              accum_out=rsum[:, n % 4, 2 * a + b:2 * a + b + 1]).then_inc(S["exp_done"], 1)
                    A(sm[:, n % 4, :], sm[:, n % 4, :], ACT.Exp).then_inc(S["exp_done"], 1)
                i = s - (AT["ga", 0] + 2)
                if 0 <= i < KT:
                    act.wait_ge(S["y_done"], i + 1)
                    A(yh[:, i, :], q_sb[:, i, :], ACT.Copy).then_inc(S["y_hi"], 1)
            for t in range(NPROJ + 4, NPROJ + KT):
                split(t)
            for t in range(NT):
                act.wait_ge(S["ln_sqrt_in"], t + 1)
                A(rstd[:, :], aggr[:, 1:2], ACT.Sqrt, bias=epst[:, 0:1]).then_inc(S["ln_sqrt"], 1)
                act.wait_ge(S["u2T_ps"], t + 1)
                if t >= 1:
                    act.wait_ge(S["logits_ps"], t)
                A(u2T[:, :, :], psum[:, 4:6, :].rearrange("p a (k n) -> p (a k) n", k=4), ACT.Copy)\
                    .then_inc(S["u2T_sb"], 1)
            act.wait_ge(S["rt_exp_in"], 1)
            A(sc[:, :, :], lg_[:, :, :], ACT.Exp).then_inc(S["rt_exp"], 1)

            def hi(b, ch):
                act.wait_ge(mraw_in[ch], (b + 1) * 16)
                act.wait_ge(S["chunk_used"], b * CH + ch + 1)
                v = mhi[ch % HLR]
                A(v[:, :, :], mraw[ch][:, :].rearrange("p (k f) -> p k f", k=2), ACT.Copy).then_inc(S["mhi_done"], 1)

            def x_hi(b):
                act.wait_ge(S["xT_m_ps"], b + 1)
                for a in range(2):
                    A(xTh[:, 4 * a:4 * a + 4, :], psum[:, 2 + a, :].rearrange("p (k n) -> p k n", k=4), ACT.Copy)\
                        .then_inc(S["xTh_m"], 1)

            def act_block(b):
                for ch in range(4):
                    hi(b, ch)
                for ch in range(4, CH):
                    hi(b, ch)
                    if ch == 7:
                        act.wait_ge(S["chunk_used"], b * CH + HLR + 4)
                        A(h_sb[:, :], bank[0], ACT.Silu).then_inc(S["silu_done"], 1)
                x_hi(b + 1)
                act.wait_ge(S["hT_ps"], b + 1)
                A(hTh[:, :, :], bank[4].rearrange("p (k n) -> p k n", k=FT), ACT.Copy).then_inc(S["hTh_done"], 1)

            x_hi(0)
            act.wait_ge(S["wout_ps"], 2 * NT)
            act_block(0)
            with act.Fori(1, NE) as b:
                act_block(b)
            act.wait_ge(S["ctrl_done"], 1)
            nblk = act.value_load(ctrl[0:1, NOVER:NOVER + 1], min_val=NE, max_val=NBLK)
            with act.If(nblk > NE):
                with act.Fori(NE, nblk) as b:
                    act_block(b)
            for t in range(NT):
                f = fin[t % 2]
                act.wait_ge(S["fin_z"], t + 1)
                A(rstd[:, :], aggr[:, 1:2], ACT.Sqrt, bias=epst[:, 0:1]).then_inc(S["ln_sqrt"], 1)

        @block.vector
        def _(dve):
            V = nc.vector
            n_order = [0]

            def mark(ins):
                n_order[0] += 1
                ins.then_inc(S["dve_order"], 1)
                return n_order[0]

            def chain(ins):
                dve.wait_ge(S["dve_order"], mark(ins))

            V.memset(ones[:, :], 1.0).then_inc(S["setup_done"], 1)
            V.memset(rbs[NBUCKET:NBUCKET + 1, :], 1.0).then_inc(S["setup_done"], 1)
            V.memset(xpad[:, 0:3], 0.0).then_inc(S["setup_done"], 1)
            V.memset(epst[:, :], EPS).then_inc(S["setup_done"], 1)
            dve.wait_ge(S["pcol_sb"], 1)
            lam = pcol[:, 56:64]
            chain(V.tensor_scalar(tiny[:, 2, :], lam, -1.0, None, ALU.mult))
            chain(V.tensor_tensor(tiny[:, 1, :], tiny[:, 2, :], lam, ALU.min))
            dve.wait_ge(S["exp_small"], 1)
            chain(V.tensor_scalar(tiny[:, 0, :], tiny[:, 0, :], 1.0, None, ALU.add))
            chain(V.reciprocal(tiny[:, 0, :], tiny[:, 0, :]))
            V.tensor_tensor(cact[:, :], ccol[:, :], tiny[:, 0, :], ALU.mult).then_inc(S["c_done"], 1)
            dve.wait_ge(S["exp_small"], 2)
            chain(V.tensor_scalar(tiny[:, 3, :], tiny[:, 1, :], 2.0, None, ALU.add))
            chain(V.reciprocal(tiny[:, 3, :], tiny[:, 3, :]))
            chain(V.tensor_tensor(tiny[:, 3, :], tiny[:, 3, :], tiny[:, 1, :], ALU.mult))
            chain(V.tensor_tensor(tiny[:, 4, :], tiny[:, 3, :], tiny[:, 3, :], ALU.mult))
            chain(V.tensor_scalar(tiny[:, 5, :], tiny[:, 4, :], 1.0 / 19, 1.0 / 17, ALU.mult, ALU.add))
            for m in (15, 13, 11, 9, 7, 5, 3, 1):
                chain(V.tensor_tensor(tiny[:, 5, :], tiny[:, 5, :], tiny[:, 4, :], ALU.mult))
                chain(V.tensor_scalar(tiny[:, 5, :], tiny[:, 5, :], 1.0 / m, None, ALU.add))
            chain(V.scalar_tensor_tensor(tiny[:, 5, :], tiny[:, 5, :], 2.0, tiny[:, 3, :], ALU.mult, ALU.mult))
            chain(V.scalar_tensor_tensor(tiny[:, 5, :], tiny[:, 2, :], 0.0, tiny[:, 5, :], ALU.max, ALU.add))
            mark(V.tensor_scalar(k8[:, :], tiny[:, 5, :], LRU_C, None, ALU.mult))
            mark(V.tensor_scalar(nk8[:, :], tiny[:, 5, :], -LRU_C, None, ALU.mult))
            mark(V.tensor_scalar(nba[:, :], pcol[:, 40:48], -1.0, None, ALU.mult))
            mark(V.tensor_scalar(hbx[:, :], pcol[:, 48:56], 0.5, None, ALU.mult))
            dve.wait_ge(S["setup_done"], 4)
            dve.wait_ge(S["pool_in"], 16 * 5)
            chain(V.tensor_copy(sinkp[:, :].rearrange("p (g a b) -> p g a b", g=4, a=2),
                                sinkt[:, :].rearrange("p (g b a) -> p g a b", g=4, a=2)))
            dve.wait_ge(S["mod1_ps"], 1)
            V.tensor_copy(mod1[:, 0:8], bank[4][:, 0:8]).then_inc(S["mod1_sb"], 1)
            chain(V.tensor_scalar(mod1[:, 8:16], bank[4][:, 8:16], 1.0, None, ALU.add))
            dve.wait_ge(S["mod1_sb"], 1)

            def split(t):
                dve.wait_ge(S["split_hi"], t + 1)
                if t < NPROJ:
                    r3 = raw[t % 3][:, :].rearrange("p (k n) -> p k n", k=KT)
                    V.tensor_tensor(wlo[t % 3][:, :, :], r3, whi[t % 3][:, :, :].bitcast(F32), ALU.subtract)\
                        .then_inc(S["split_lo"], 1)
                else:
                    k = t - NPROJ
                    V.tensor_tensor(wol[k][:, :], raw[t % 3][:, :], woh[k][:, :].bitcast(F32), ALU.subtract)\
                        .then_inc(S["split_lo"], 1)

            split(0)
            split(1)
            for k in range(KT):
                dve.wait_ge(S["xT_sb"], k + 1)
                V.tensor_scalar(xT[:, k, :], xT[:, k, :], mod1[:, 8 + k:9 + k], mod1[:, k:k + 1],
                                ALU.mult, ALU.add).then_inc(S["mod1_sb"], 1)
                if k >= 1:
                    dve.wait_ge(S["u_hi"], k)
                    V.tensor_tensor(ul[:, k - 1, :], xT[:, k - 1, :], uh[:, k - 1, :].bitcast(F32),
                                    ALU.subtract).then_inc(S["u_lo"], 1)
            dve.wait_ge(S["u_hi"], KT)
            V.tensor_tensor(ul[:, KT - 1, :], xT[:, KT - 1, :], uh[:, KT - 1, :].bitcast(F32),
                            ALU.subtract).then_inc(S["u_lo"], 1)
            dve.wait_ge(S["u_lo"], KT)

            for s in range(NPROJ + 2):
                if s + 2 < NPROJ + KT:
                    split(s + 2)
                n = UNIT_AT.get(s - 1)
                if n is not None:
                    hg, first = n // 4, n % 4 == 0
                    lo = P if first else 0
                    r, sl = n % 4, ssb[n % 2][:, :, :, lo:256]
                    dve.wait_ge(S["sc_ps"], n + 1)
                    dve.wait_ge(bias_in[hg % 2], 32 * (hg // 2 + 1))
                    if n >= 2:
                        dve.wait_ge(S["pt_ps"], n - 1)
                    for a in range(2):
                        k_ = mark(V.tensor_tensor(ssb[n % 2][:, a, :, lo:256], scores[:, a, :, lo:256],
                                                  bias[hg % 2][:, a, :, lo:256], ALU.add))
                    dve.wait_ge(S["dve_order"], k_)
                    chain(V.tensor_reduce(mx[:, r, :].rearrange("p (a b) -> p a b", a=2), sl, AX.X, ALU.max))
                    chain(V.tensor_tensor(mx[:, r, :], mx[:, r, :], sinkp[:, 4 * hg:4 * hg + 4], ALU.max))
                    if n >= 4:
                        dve.wait_ge(S["on_done"], n - 3)
                    k_ = mark(V.tensor_scalar(negm[:, r, :], mx[:, r, :], -1.0, None, ALU.mult))
                    dve.wait_ge(S["dve_order"], k_)
                    V.tensor_tensor(sm[:, r, :], sinkp[:, 4 * hg:4 * hg + 4], mx[:, r, :], ALU.subtract)\
                        .then_inc(S["logit_done"], 1)
                n = UNIT_AT.get(s - 4)
                if n is not None:
                    r = n % 4
                    dve.wait_ge(S["exp_done"], 5 * (n + 1))
                    chain(V.tensor_tensor(rden[:, r, :], rsum[:, r, :], sm[:, r, :], ALU.add))
                    chain(V.reciprocal(rden[:, r, :], rden[:, r, :]))
                    dve.wait_ge(S["o_ps"], n + 1)
                    if n >= 1:
                        dve.wait_ge(S["ot_ps"], n)
                    for b in range(2):
                        ins = V.tensor_tensor(
                            onrm[:, b * P:(b + 1) * P].rearrange("p (a d) -> p a d", a=2),
                            bank[6][:, b * P:(b + 1) * P].rearrange("p (a d) -> p a d", a=2),
                            rden[:, r, b:4:2].unsqueeze(2).to_broadcast([P, 2, HD]), ALU.mult)
                        if b == 0:
                            mark(ins)
                        else:
                            ins.then_inc(S["on_done"], 1)
                i = s - 5
                if 0 <= i < KT:
                    dve.wait_ge(S["er_done"], i + 1)
                    chain(V.tensor_scalar(dec[:, i, :], dec[:, i, :], 1.0, None, ALU.add))
                    V.reciprocal(dec[:, i, :], dec[:, i, :]).then_inc(S["r_done"], 1)
                    dve.wait_ge(S["ti_done"], i + 1)
                    V.scalar_tensor_tensor(ix[:, i, :], ix[:, i, :], 1.0, xc[i % 2][:, :], ALU.add, ALU.mult)\
                        .then_inc(S["ix_done"], 1)
                i = s - 3
                if 0 <= i < KT:
                    dve.wait_ge(S["evac"], AT["lx", i] + 1)
                    v = xc[i % 2]
                    if i >= 2:
                        dve.wait_ge(S["li_ps"], i - 1)
                        dve.wait_ge(S["ix_done"], i - 1)
                    chain(V.tensor_scalar(v[:, :], xpad[:, 0:T], pcol[:, i:i + 1], pcol[:, 32 + i:33 + i],
                                          ALU.mult, ALU.add))
                    for j in range(1, 4):
                        ins = V.scalar_tensor_tensor(v[:, :], xpad[:, j:j + T], pcol[:, 8 * j + i:8 * j + i + 1],
                                                     v[:, :], ALU.mult, ALU.add)
                        if j < 3:
                            chain(ins)
                        else:
                            ins.then_inc(S["conv_done"], 1)
                i = s - 7
                if 0 <= i < KT:
                    dve.wait_ge(S["ta_done"], i + 1)
                    chain(V.tensor_scalar(yb[:, i, :], tt[i % 2][:, :], 1.0, None, ALU.add))
                    chain(V.reciprocal(yb[:, i, :], yb[:, i, :]))
                    V.scalar_tensor_tensor(yb[:, i, :], tt[i % 2][:, :], 2.0, yb[:, i, :], ALU.mult, ALU.mult)\
                        .then_inc(S["m2_done"], 1)
                i = s - 16
                if 0 <= i < KT:
                    dve.wait_ge(S["sqrt_done"], 1)
                    dve.wait_ge(S["ix_done"], i + 1)
                    chain(V.scalar_tensor_tensor(ix[:, i, :], ix[:, i, :], 0.5, yb[:, i, :], ALU.mult, ALU.mult))
                    V.tensor_tensor_scan(yb[:, i, :], dec[:, i, :], ix[:, i, :], 0.0, ALU.mult, ALU.add)\
                        .then_inc(S["h_done"], 1)
                i = s - (AT["lg", 0] + 1)
                if 0 <= i < KT:
                    dve.wait_ge(S["sq_done"], i + 1)
                    chain(V.tensor_scalar(gt[i % 2][:, :], gt[i % 2][:, :], 0.044715, 1.0, ALU.mult, ALU.add))
                    dve.wait_ge(S["evac"], AT["lg", i] + 1)
                    V.tensor_tensor(gt[i % 2][:, :], gt[i % 2][:, :], xg[i % 2][:, :], ALU.mult).then_inc(S["g_arg"], 1)
                i = s - (AT["lg", 0] + 2)
                if 0 <= i < KT:
                    dve.wait_ge(S["g_tanh"], i + 1)
                    dve.wait_ge(S["h_done"], i + 1)
                    chain(V.scalar_tensor_tensor(gt[i % 2][:, :], gt[i % 2][:, :], 1.0, xg[i % 2][:, :], ALU.add, ALU.mult))
                    V.scalar_tensor_tensor(yb[:, i, :], gt[i % 2][:, :], 0.5, yb[:, i, :], ALU.mult, ALU.mult)\
                        .then_inc(S["gelu_done"], 1)
                i = s - (AT["gb", 0] + 1)
                if 0 <= i < KT:
                    dve.wait_ge(S["evac"], AT["gb", i] + 1)
                    dve.wait_ge(S["gelu_done"], i + 1)
                    V.scalar_tensor_tensor(yb[:, i, :], gt[i % 2][:, :], 1.0, yb[:, i, :], ALU.add, ALU.mult)\
                        .then_inc(S["yb_done"], 1)
                i = s - (AT["ga", 0] + 1)
                if 0 <= i < KT:
                    dve.wait_ge(S["evac"], AT["ga", i] + 1)
                    dve.wait_ge(S["ya_done"], 4 * (i // 2 + 1))
                    dve.wait_ge(S["yb_done"], i + 1)
                    chain(V.scalar_tensor_tensor(q_sb[:, i, :], gt[i % 2][:, :], 1.0, q_sb[:, i, :], ALU.add, ALU.mult))
                    V.tensor_tensor(q_sb[:, i, :], q_sb[:, i, :], yb[:, i, :], ALU.add).then_inc(S["y_done"], 1)
                i = s - (AT["ga", 0] + 2)
                if 0 <= i < KT:
                    dve.wait_ge(S["y_hi"], i + 1)
                    dve.wait_ge(S["y_done"], i + 1)
                    V.tensor_tensor(yl[:, i, :], q_sb[:, i, :], yh[:, i, :].bitcast(F32), ALU.subtract)\
                        .then_inc(S["y_lo"], 1)
                if s == 29:
                    dve.wait_ge(S["mod2_ps"], 1)
                    V.tensor_copy(mod2c[:, :], bank[7][:, 256:288]).then_inc(S["mod2_sb"], 1)
                if s == 32:
                    dve.wait_ge(S["mod2_T"], 1)
                    V.tensor_copy(mod2r[:, :], psum[0:32, 7, 256:384]).then_inc(S["mod2_row"], 1)
            for t in range(NPROJ + 4, NPROJ + KT):
                split(t)

            dve.wait_ge(S["rows_ready"], 1)
            dve.wait_ge(x1_in, 16 * NT)
            for t in range(NT):
                b0 = 2 * (t % 2)
                yv = psum[:, b0:b0 + 2, :].rearrange("p a n -> p (a n)")
                dve.wait_ge(S["wout_ps"], 2 * (t + 1))
                if t >= 1:
                    dve.wait_ge(S["xn_used"], t)
                    dve.wait_ge(S["u2_done"], t)
                V.tensor_tensor(zt[:, :], yv, gate1r[:, :], ALU.mult).then_inc(S["fin_n"], 1)
                dve.wait_ge(S["fin_n"], t + 1)
                chain(V.scalar_tensor_tensor(zt[:, :], x1[:, t, :], ALPHA, zt[:, :], ALU.mult, ALU.add))
                for a in range(2):
                    k_ = mark(V.bn_stats(stats[:, a, :], zt[:, a * 512:(a + 1) * 512]))
                dve.wait_ge(S["dve_order"], k_)
                if t >= 1:
                    dve.wait_ge(S["xn_done"], t)
                V.bn_aggr(aggr[:, :], stats[:, :, :].rearrange("p a b -> p (a b)")).then_inc(S["ln_sqrt_in"], 1)
                dve.wait_ge(S["ln_sqrt_in"], t + 1)
                dve.wait_ge(S["ln_sqrt"], t + 1)
                chain(V.reciprocal(rstd[:, :], rstd[:, :]))
                V.tensor_scalar(zt[:, :], zt[:, :], aggr[:, 0:1], rstd[:, 0:1], ALU.subtract, ALU.mult)\
                    .then_inc(S["xn_done"], 1)
                dve.wait_ge(S["xn_done"], t + 1)
                if t >= 2:
                    dve.wait_ge(S["u2T_ps"], t - 1)
                    dve.wait_ge(u2_st[t % 2], 16 * (t // 2))
                chain(V.tensor_tensor(u2[t % 2][:, :], zt[:, :], a2r[:, :], ALU.mult))
                V.tensor_tensor(u2[t % 2][:, :], u2[t % 2][:, :], b2r[:, :], ALU.add).then_inc(S["u2_done"], 1)

            dve.wait_ge(S["logits_ps"], NT)
            dve.wait_ge(S["wout_ps"], 2 * NT)
            lgp = bank[6][:, 0:64].rearrange("p (t e) -> p t e", t=NT)
            b3 = [P, NT, NE]
            r4 = red[:, 0, :]
            chain(V.tensor_reduce(r4, lgp, AX.X, ALU.max))
            V.tensor_tensor(lg_[:, :, :], lgp, r4.unsqueeze(2).to_broadcast(b3), ALU.subtract).then_inc(S["rt_exp_in"], 1)
            dve.wait_ge(S["rt_exp"], 1)
            chain(V.tensor_reduce(red[:, 1, :], sc[:, :, :], AX.X, ALU.add))
            chain(V.reciprocal(red[:, 1, :], red[:, 1, :]))
            chain(V.tensor_tensor(sc[:, :, :], sc[:, :, :], red[:, 1, :].unsqueeze(2).to_broadcast(b3), ALU.mult))

            def ranks(out3, in3, n):
                i_of = in3.unsqueeze(3).to_broadcast([P, n, 4, 4])
                j_of = in3.unsqueeze(2).to_broadcast([P, n, 4, 4])
                ge = cge[:, 0:16 * n].rearrange("p (g i j) -> p g i j", i=4, j=4)
                gtr = cgt[:, 0:16 * n].rearrange("p (g i j) -> p g i j", i=4, j=4)
                mark(V.tensor_tensor(ge, i_of, j_of, ALU.is_ge))
                chain(V.tensor_tensor(gtr, i_of, j_of, ALU.is_gt))
                f1 = cge[:, 0:16 * n].rearrange("p (g m) -> p g m", m=16)
                f2 = cgt[:, 0:16 * n].rearrange("p (g m) -> p g m", m=16)
                mark(V.tensor_tensor(f1, f1, cst[:, C_LT:C_LT + 16].unsqueeze(1).to_broadcast([P, n, 16]), ALU.mult))
                chain(V.tensor_tensor(f2, f2, cst[:, C_GT:C_GT + 16].unsqueeze(1).to_broadcast([P, n, 16]), ALU.mult))
                chain(V.tensor_tensor(cge[:, 0:16 * n], cge[:, 0:16 * n], cgt[:, 0:16 * n], ALU.add))
                chain(V.tensor_reduce(out3, cge[:, 0:16 * n].rearrange("p (g i j) -> p g j i", i=4, j=4), AX.X, ALU.add))

            sc3 = sc[:, :, :].rearrange("p t (g e) -> p (t g) e", g=GRP)
            ranks(rank[:, :, :], sc3, 16)
            chain(V.tensor_scalar(sel[:, :, :], rank[:, :, :], 2.0, None, ALU.is_lt))
            chain(V.tensor_tensor(sel[:, :, :], sel[:, :, :], sc3, ALU.mult))
            chain(V.tensor_reduce(gsc[:, :, :].rearrange("p t g -> p (t g)"), sel[:, :, :], AX.X, ALU.add))
            ranks(grank[:, :, :], gsc[:, :, :], 4)
            chain(V.tensor_scalar(grank[:, :, :], grank[:, :, :], 0.0, None, ALU.is_equal))
            gb_ = grank[:, :, :].rearrange("p t g -> p (t g)").unsqueeze(2).to_broadcast([P, 16, 4])
            R = [r0, r1]
            for r in range(2):
                v = R[r][:, :, :].rearrange("p t (g e) -> p (t g) e", g=GRP)
                chain(V.tensor_scalar(v, rank[:, :, :], float(r), None, ALU.is_equal))
                chain(V.tensor_tensor(v, v, gb_, ALU.mult))
            chain(V.tensor_tensor(mm[:, :, :], r0[:, :, :], r1[:, :, :], ALU.add))
            mark(V.memset(mpre[:, 0, :], 0.0))
            chain(V.tensor_copy(mpre[:, 1, :], mm[:, 0, :]))
            chain(V.tensor_tensor(mpre[:, 2, :], mpre[:, 1, :], mm[:, 1, :], ALU.add))
            chain(V.tensor_tensor(mpre[:, 3, :], mpre[:, 2, :], mm[:, 2, :], ALU.add))
            V.tensor_tensor(mtot[:, :], mpre[:, 3, :], mm[:, 3, :], ALU.add).then_inc(S["m_done"], 1)
            for r in range(2):
                chain(V.tensor_tensor(t64[:, :, :], R[r][:, :, :], sc[:, :, :], ALU.mult))
                chain(V.tensor_reduce(red[:, 2 + r, :], t64[:, :, :], AX.X, ALU.add))
            chain(V.tensor_tensor(red[:, 4, :], red[:, 2, :], red[:, 3, :], ALU.add))
            chain(V.reciprocal(red[:, 4, :], red[:, 4, :]))
            mark(V.tensor_tensor(wA[:, :], red[:, 2, :], red[:, 4, :], ALU.mult))
            mark(V.tensor_tensor(wB[:, :], red[:, 3, :], red[:, 4, :], ALU.mult))
            chain(V.tensor_copy(tokid[:, :], cst[:, C_TOK:C_TOK + NT]))
            dve.wait_ge(S["pos_ps"], 1)
            mark(V.tensor_copy(pos[:, :, :], bank[7][:, 0:64].rearrange("p (t e) -> p t e", t=NT)))
            chain(V.tensor_copy(cnt[:, :], bank[7][:, 64:80]))
            chain(V.tensor_scalar(qq[:, :, :], pos[:, :, :], 128.0, None, ALU.is_ge))
            chain(V.scalar_tensor_tensor(qq[:, :, :], pos[:, :, :], 256.0, qq[:, :, :], ALU.is_ge, ALU.add))
            chain(V.scalar_tensor_tensor(qq[:, :, :], pos[:, :, :], 384.0, qq[:, :, :], ALU.is_ge, ALU.add))
            chain(V.scalar_tensor_tensor(pos[:, :, :], qq[:, :, :], -128.0, pos[:, :, :], ALU.mult, ALU.add))
            chain(V.tensor_scalar(ovc[:, :], cnt[:, :], 129.0, None, ALU.is_ge))
            chain(V.scalar_tensor_tensor(ovc[:, :], cnt[:, :], 257.0, ovc[:, :], ALU.is_ge, ALU.add))
            chain(V.scalar_tensor_tensor(ovc[:, :], cnt[:, :], 385.0, ovc[:, :], ALU.is_ge, ALU.add))
            chain(V.tensor_tensor_scan(ovi[:, :], ones[:, 0:NE], ovc[:, :], 0.0, ALU.mult, ALU.add))
            chain(V.tensor_tensor(ovs[:, :], ovi[:, :], ovc[:, :], ALU.subtract))
            ebc = cst[:, C_EXP:C_EXP + NE].unsqueeze(1).to_broadcast(b3)
            chain(V.tensor_tensor(blk[:, :, :], qq[:, :, :], ovs[:, :].unsqueeze(1).to_broadcast(b3), ALU.add))
            chain(V.scalar_tensor_tensor(blk[:, :, :], blk[:, :, :], 15.0, ebc, ALU.add, ALU.subtract))
            chain(V.tensor_scalar(t64[:, :, :], qq[:, :, :], 1.0, None, ALU.min))
            chain(V.tensor_tensor(blk[:, :, :], blk[:, :, :], t64[:, :, :], ALU.mult))
            chain(V.tensor_tensor(blk[:, :, :], blk[:, :, :], ebc, ALU.add))
            chain(V.scalar_tensor_tensor(tb[:, :, :], pos[:, :, :], float(TCOL), blk[:, :, :], ALU.mult, ALU.add))
            chain(V.scalar_tensor_tensor(qq[:, :, :], blk[:, :, :], float(P), pos[:, :, :], ALU.mult, ALU.add))
            for r in range(2):
                chain(V.tensor_tensor(t64[:, :, :], R[r][:, :, :], tb[:, :, :], ALU.mult))
                chain(V.tensor_reduce(red[:, 4 + r, :], t64[:, :, :], AX.X, ALU.add))
            V.tensor_copy(tslot[:, :, :], red[:, 4:6, :]).then_inc(S["slots_done"], 1)
            for r in range(2):
                chain(V.tensor_tensor(t64[:, :, :], R[r][:, :, :], qq[:, :, :], ALU.mult))
                chain(V.tensor_reduce(red[:, 6 + r, :], t64[:, :, :], AX.X, ALU.add))
            chain(V.tensor_copy(yrow[:, :, :], red[:, 6:8, :]))
            b7 = [P, NOVER, NE]
            jb = cst[:, C_J:C_J + NOVER].unsqueeze(2).to_broadcast(b7)
            chain(V.tensor_tensor(own[:, :, :], ovs[:, :].unsqueeze(1).to_broadcast(b7), jb, ALU.is_le))
            chain(V.tensor_tensor(own2[:, :, :], ovi[:, :].unsqueeze(1).to_broadcast(b7), jb, ALU.is_gt))
            chain(V.tensor_tensor(own[:, :, :], own[:, :, :], own2[:, :, :], ALU.mult))
            chain(V.tensor_tensor(own[:, :, :], own[:, :, :],
                                  cst[:, C_EXP:C_EXP + NE].unsqueeze(1).to_broadcast(b7), ALU.mult))
            chain(V.tensor_reduce(ctrlf[:, 0:NOVER], own[:, :, :], AX.X, ALU.add))
            chain(V.tensor_scalar(ctrlf[:, NOVER:NOVER + 1], ovi[:, NE - 1:NE], float(NE), None, ALU.add))
            chain(V.tensor_scalar(ctrlf[:, NOVER + 1:NOVER + 2], ovi[:, NE - 1:NE], float(NE - 1), None, ALU.add))
            V.tensor_copy(ctrl[:, :], ctrlf[:, :]).then_inc(S["ctrl_done"], 1)

            def lo(b, ch):
                dve.wait_ge(S["mhi_done"], b * CH + ch + 1)
                V.tensor_tensor(mlo[ch % HLR][:, :, :], mraw[ch][:, :].rearrange("p (k f) -> p k f", k=2),
                                mhi[ch % HLR][:, :, :].bitcast(F32), ALU.subtract).then_inc(S["mlo_done"], 1)

            def x_lo(b):
                for a in range(2):
                    dve.wait_ge(S["xTh_m"], 2 * b + a + 1)
                    V.tensor_tensor(xTl[:, 4 * a:4 * a + 4, :], psum[:, 2 + a, :].rearrange("p (k n) -> p k n", k=4),
                                    xTh[:, 4 * a:4 * a + 4, :].bitcast(F32), ALU.subtract).then_inc(S["xTl_m"], 1)

            def y_out(b, first=False):
                dve.wait_ge(S["chunk_used"], b * CH + HLR + CH)
                if not first:
                    dve.wait_ge(S["y_st"], b * 16)
                for a in range(2):
                    V.tensor_tensor(ysb[:, a * 512:(a + 1) * 512], bank[5 + a], gate2r[:, a * 512:(a + 1) * 512],
                                    ALU.mult).then_inc(S["y_ev0" if a == 0 else "y_ev1"], 1)

            def dve_block(b, first, second=False):
                for ch in range(4):
                    lo(b, ch)
                if not first:
                    y_out(b - 1, first=second)
                for ch in range(4, CH):
                    lo(b, ch)
                dve.wait_ge(S["chunk_used"], b * CH + HLR + 8)
                dve.wait_ge(S["silu_done"], b + 1)
                V.tensor_tensor(h_sb[:, :], h_sb[:, :], bank[1], ALU.mult).then_inc(S["h_done_m"], 1)
                x_lo(b + 1)
                dve.wait_ge(S["hTh_done"], b + 1)
                V.tensor_tensor(hTl[:, :, :], bank[4].rearrange("p (k n) -> p k n", k=FT),
                                hTh[:, :, :].bitcast(F32), ALU.subtract).then_inc(S["hTl_done"], 1)

            x_lo(0)
            dve.wait_ge(rows_in, 16 * 8)
            dve_block(0, True)
            dve_block(1, False, second=True)
            with dve.Fori(2, NE) as b:
                dve_block(b, False)
            dve.wait_ge(S["ctrl_done"], 1)
            nblk = dve.value_load(ctrl[0:1, NOVER:NOVER + 1], min_val=NE, max_val=NBLK)
            with dve.If(nblk > NE):
                with dve.Fori(NE, nblk) as b:
                    dve_block(b, False)
            last = dve.value_load(ctrl[0:1, NOVER + 1:NOVER + 2], min_val=NE - 1, max_val=NBLK - 1)
            y_out(last)

            for t in range(NT):
                z, ya_, yb_ = fin[t % 2]
                dve.wait_ge(fgather[t % 2], 32 * (t // 2 + 1))
                dve.wait_ge(S["x1_done"], NT)
                if t >= 2:
                    dve.wait_ge(out_st[t % 2], 16 * (t // 2))
                chain(V.scalar_tensor_tensor(z[:, :], ya_[:, :], wA[:, t:t + 1], x1[:, t, :], ALU.mult, ALU.add))
                chain(V.scalar_tensor_tensor(z[:, :], yb_[:, :], wB[:, t:t + 1], z[:, :], ALU.mult, ALU.add))
                for a in range(2):
                    k_ = mark(V.bn_stats(stats[:, a, :], z[:, a * 512:(a + 1) * 512]))
                dve.wait_ge(S["dve_order"], k_)
                V.bn_aggr(aggr[:, :], stats[:, :, :].rearrange("p a b -> p (a b)")).then_inc(S["fin_z"], 1)
                dve.wait_ge(S["fin_z"], t + 1)
                dve.wait_ge(S["ln_sqrt"], NT + t + 1)
                chain(V.reciprocal(rstd[:, :], rstd[:, :]))
                chain(V.tensor_scalar(z[:, :], z[:, :], aggr[:, 0:1], rstd[:, 0:1], ALU.subtract, ALU.mult))
                chain(V.tensor_tensor(z[:, :], z[:, :], g2r[:, :], ALU.mult))
                V.tensor_tensor(z[:, :], z[:, :], be2r[:, :], ALU.add).then_inc(S["fin_out"], 1)

        @block.tensor
        def _(pe):
            mmul = nc.tensor.matmul
            pe.sem_inc(S["chunk_used"], HLR)
            pe.wait_ge(const_in, 16)
            pe.wait_ge(param_in, 16 * 5)
            nc.tensor.transpose(bank[7][:, 0:64], prm[:, :], ident[0:64, 0:64]).then_inc(S["pcol_ps"], 1)
            pe.wait_ge(S["setup_done"], 4)
            pe.wait_ge(S["pool_in"], 16 * 5)
            mmul(psum[0:NQ, 6, 0:384], rbs[:, :], cst[0:NBUCKET + 1, C_HOT:C_HOT + 384], start=True, stop=True)\
                .then_inc(S["bvec_ps"], 1)
            pe.wait_ge(x_in, 16 * NT)
            for k in range(KT):
                if k >= 4:
                    pe.wait_ge(S["xT_sb"], k - 3)
                for t in range(NT):
                    ins = nc.tensor.transpose(bank[k % 4][:, t * P:(t + 1) * P], x_sb[:, t, k * P:(k + 1) * P], ident)
                ins.then_inc(S["xT_ps"], 1)
            pe.wait_ge(small_in, 32)
            pe.wait_ge(S["c_done"], 1)
            for j in range(8):
                pe.wait_ge(ada1_sem[j], 16)
                for n in range(16):
                    ins = mmul(bank[4][:, n:n + 1], ada1[:, j, n * P:(n + 1) * P], cact[:, j:j + 1],
                               start=(j == 0 and n == 0), stop=False, skip_group_check=True)
            mmul(bank[4][:, 0:16], adab1[:, :], ident[0:16, 0:16], start=False, stop=True,
                 skip_group_check=True).then_inc(S["mod1_ps"], 1)

            def project(s):
                kind = TILES[s][0]
                h, l = whi[s % 3], wlo[s % 3]
                pe.wait_ge(S["split_lo"], s + 1)
                if s >= 2:
                    pe.wait_ge(S["evac"], s - 1)
                else:
                    pe.wait_ge(S["xT_sb"], KT)
                if kind == "v":
                    for t in range(NT):
                        o_ = bank[s % 2][:, t * P:(t + 1) * P]
                        for k in range(KT):
                            a, b = uh[:, k, t * P:(t + 1) * P], ul[:, k, t * P:(t + 1) * P]
                            mmul(o_, a, h[:, k, :], start=(k == 0), stop=False)
                            mmul(o_, a, l[:, k, :], start=False, stop=False)
                            ins = mmul(o_, b, h[:, k, :], start=False, stop=(k == KT - 1))
                else:
                    for k in range(KT):
                        if s == 0:
                            pe.wait_ge(S["u_lo"], k + 1)
                        mmul(bank[s % 2], h[:, k, :], uh[:, k, :], start=(k == 0), stop=False)
                        mmul(bank[s % 2], h[:, k, :], ul[:, k, :], start=False, stop=False)
                        ins = mmul(bank[s % 2], l[:, k, :], uh[:, k, :], start=False, stop=(k == KT - 1))
                ins.then_inc(S["proj_ps"], 1)

            for s in range(NPROJ):
                project(s)
                n = UNIT_AT.get(s - 4)
                if n is not None:
                    pe.wait_ge(S["on_done"], n + 1)
                    if n >= 1:
                        pe.wait_ge(S["ya_done"], n)
                    if s == 29:
                        pe.wait_ge(S["mod2_sb"], 1)
                    if s == 32:
                        pe.wait_ge(S["mod2_row"], 1)
                    for a in range(2):
                        ins = nc.tensor.transpose(bank[7][:, a * P:(a + 1) * P], onrm[:, a * P:(a + 1) * P], ident)
                    ins.then_inc(S["ot_ps"], 1)
                n = UNIT_AT.get(s - 3)
                if n is not None:
                    blk_, kv = n % 4, n // 8
                    pe.wait_ge(S["pt_sb"], n + 1)
                    if n >= 1:
                        pe.wait_ge(S["on_done"], n)
                    for a in range(2):
                        for b in range(2):
                            hh = 2 * b + a
                            halves = [1] if blk_ == 0 else [0, 1]
                            for half in halves:
                                ins = mmul(bank[6][:, hh * HD:(hh + 1) * HD], ptb[:, a, b, half, :],
                                           vv[:, blk_ - 1 + half, kv * HD:(kv + 1) * HD],
                                           start=(half == halves[0]), stop=(half == 1))
                    ins.then_inc(S["o_ps"], 1)
                n = UNIT_AT.get(s - 2)
                if n is not None:
                    pe.wait_ge(S["exp_done"], 5 * (n + 1))
                    if n >= 1:
                        pe.wait_ge(S["pt_sb"], n)
                    for a in range(2):
                        for b in range(2):
                            for half in ([1] if n % 4 == 0 else [0, 1]):
                                ins = nc.tensor.transpose(ptps[:, a, b, half, :],
                                                          ssb[n % 2][:, a, b, half * P:(half + 1) * P], ident)
                    ins.then_inc(S["pt_ps"], 1)
                n = UNIT_AT.get(s)
                if n is not None:
                    hg, blk_ = n // 4, n % 4
                    lo_ = P if blk_ == 0 else 0
                    pe.wait_ge(S["evac"], AT["q", 2 * hg + 1] + 1)
                    pe.wait_ge(kdup_in, 32)
                    if n >= 1:
                        pe.wait_ge(S["logit_done"], n)
                    for b in range(2):
                        for a in range(2):
                            rows_ = slice(64 * a, 64 * a + 64)
                            ins = mmul(scores[:, a, b, lo_:256], q_sb[rows_, 2 * hg + b, blk_ * P:(blk_ + 1) * P],
                                       kk[hg // 2][rows_, blk_ * P - P + lo_:(blk_ + 1) * P], start=True, stop=True)
                    ins.then_inc(S["sc_ps"], 1)
                i = s - 4
                if 0 <= i < KT:
                    pe.wait_ge(S["conv_done"], i + 1)
                    pe.wait_ge(lruw_in, 32)
                    if i >= 1:
                        pe.wait_ge(S["er_done"], i)
                        pe.wait_ge(S["ti_done"], i)
                    mmul(bank[6], wax[:, 0, i, :], xc[i % 2][:, :], start=True, stop=True).then_inc(S["lr_ps"], 1)
                    mmul(bank[7], wax[:, 1, i, :], xc[i % 2][:, :], start=True, stop=True).then_inc(S["li_ps"], 1)
                if s == 28:
                    pe.wait_ge(S["ada2_used"], 16)
                    pe.wait_ge(S["ya_done"], max(n for n in range(NU) if START[n] + 4 <= s) + 1)
                    for n in range(32):
                        ins = mmul(bank[7][:, 256 + n:257 + n], acc2[:, n * P:(n + 1) * P], ones[:, 0:1],
                                   start=(n == 0), stop=False, skip_group_check=True)
                    mmul(bank[7][:, 256:288], adab2[:, :], ident[0:32, 0:32], start=False, stop=True,
                         skip_group_check=True).then_inc(S["mod2_ps"], 1)
                if s == 31:
                    pe.wait_ge(S["mod2_sb"], 1)
                    pe.wait_ge(S["ya_done"], max(n for n in range(NU) if START[n] + 4 <= s) + 1)
                    nc.tensor.transpose(psum[0:32, 7, 256:384], mod2c[:, :], ident).then_inc(S["mod2_T"], 1)

            def to_router(t):
                pe.wait_ge(S["u2_done"], t + 1)
                if t >= 1:
                    pe.wait_ge(S["u2T_sb"], t)
                for k in range(KT):
                    ins = nc.tensor.transpose(psum[:, 4 + k // 4, (k % 4) * P:(k % 4 + 1) * P],
                                              u2[t % 2][:, k * P:(k + 1) * P], ident)
                ins.then_inc(S["u2T_ps"], 1)

            def logits(t):
                pe.wait_ge(S["u2T_sb"], t + 1)
                o_ = bank[6][:, t * NE:(t + 1) * NE]
                mmul(o_, ones[0:1, :], rbr[:, :], start=True, stop=False)
                for k in range(KT):
                    ins = mmul(o_, u2T[:, k, :], rw[:, k, :], start=False, stop=(k == KT - 1))
                ins.then_inc(S["logits_ps"], 1)

            for t in range(NT):
                for n in range(2):
                    o_ = bank[2 * (t % 2) + n]
                    if t == 0 and n == 0:
                        pe.wait_ge(S["y_lo"], KT)
                    if t >= 2:
                        pe.wait_ge(S["fin_n"], t - 1)
                    for k in range(KT):
                        if t == 0 and n == 0:
                            pe.wait_ge(S["split_lo"], NPROJ + k + 1)
                        a, b = yh[:, k, t * P:(t + 1) * P], yl[:, k, t * P:(t + 1) * P]
                        cols = slice(n * 512, (n + 1) * 512)
                        mmul(o_, a, woh[k][:, cols], start=(k == 0), stop=False)
                        mmul(o_, a, wol[k][:, cols], start=False, stop=False)
                        ins = mmul(o_, b, woh[k][:, cols], start=False, stop=(k == KT - 1))
                    ins.then_inc(S["wout_ps"], 1)
                    if n == 0 and t >= 1:
                        to_router(t - 1)
                    if n == 1 and t >= 1:
                        logits(t - 1)
            to_router(NT - 1)
            logits(NT - 1)
            pe.wait_ge(S["m_done"], 1)
            f = bank[7][:, 0:64]
            mmul(f, cst[:, C_LOW:C_LOW + P], mm[:, :, :].rearrange("p t e -> p (t e)"), start=True, stop=False)
            mmul(f, ones[:, :], mpre[:, :, :].rearrange("p t e -> p (t e)"), start=False, stop=True)
            mmul(bank[7][:, 64:80], ones[:, :], mtot[:, :], start=True, stop=True, skip_group_check=True)\
                .then_inc(S["pos_ps"], 1)

            def xpose(b):
                pe.wait_ge(S["gath"], (b + 1) * 16)
                for k in range(KT):
                    ins = nc.tensor.transpose(psum[:, 2 + k // 4, (k % 4) * P:(k % 4 + 1) * P],
                                              xg_m[:, k * P:(k + 1) * P], ident)
                ins.then_inc(S["xT_m_ps"], 1)

            def chunk(b, ch):
                pe.wait_ge(S["mlo_done"], b * CH + ch + 1)
                h, l = mhi[ch % HLR], mlo[ch % HLR]
                if ch < 8:
                    o_ = bank[ch // 4]
                    for i in range(2):
                        k = 2 * (ch % 4) + i
                        first, last = ch % 4 == 0 and i == 0, ch % 4 == 3 and i == 1
                        mmul(o_, xTh[:, k, :], h[:, i, :], start=first, stop=False)
                        mmul(o_, xTh[:, k, :], l[:, i, :], start=False, stop=False)
                        ins = mmul(o_, xTl[:, k, :], h[:, i, :], start=False, stop=last)
                else:
                    k = ch - 8
                    for i in range(2):
                        mmul(bank[5 + i], hTh[:, k, :], h[:, i, :], start=(k == 0), stop=False)
                        mmul(bank[5 + i], hTh[:, k, :], l[:, i, :], start=False, stop=False)
                    for i in range(2):
                        ins = mmul(bank[5 + i], hTl[:, k, :], h[:, i, :], start=False, stop=(k == FT - 1))
                ins.then_inc(S["chunk_used"], 1)

            def pe_block(b, first):
                pe.wait_ge(S["xTl_m"], 2 * b + 2)
                if not first:
                    pe.wait_ge(S["h_done_m"], b)
                for ch in range(8):
                    chunk(b, ch)
                xpose(b + 1)
                pe.wait_ge(S["h_done_m"], b + 1)
                for k in range(FT):
                    ins = nc.tensor.transpose(bank[4][:, k * P:(k + 1) * P], h_sb[:, k * P:(k + 1) * P], ident)
                ins.then_inc(S["hT_ps"], 1)
                pe.wait_ge(S["hTl_done"], b + 1)
                if not first:
                    pe.wait_ge(S["y_ev1"], b)
                    pe.wait_ge(S["y_ev0"], b)
                for ch in range(8, CH):
                    chunk(b, ch)

            xpose(0)
            pe_block(0, True)
            with pe.Fori(1, NE) as b:
                pe_block(b, False)
            pe.wait_ge(S["ctrl_done"], 1)
            nblk = pe.value_load(ctrl[0:1, NOVER:NOVER + 1], min_val=NE, max_val=NBLK)
            with pe.If(nblk > NE):
                with pe.Fori(NE, nblk) as b:
                    pe_block(b, False)


_INS = ["x", "c", "ada_w", "ada_b", "w_in", "attn_sink", "rel_bias", "conv_w", "conv_b", "lru_wa", "lru_ba",
        "lru_wx", "lru_bx", "lru_lambda", "w_out", "ln1_g", "ln1_b", "router_w", "router_b", "moe_w_gate",
        "moe_w_up", "moe_w_down", "ln2_g", "ln2_b"]


def kernel(**inputs):
    import concourse.bacc as _bacc
    from concourse.bass_utils import run_bass_kernel_spmd as _run

    nc = _bacc.Bacc("TRN2", target_bir_lowering=False, num_devices=1)
    arrays, args = {}, []
    for name in _INS + ["consts"]:
        a = constants() if name == "consts" else np.ascontiguousarray(inputs[name])
        arrays[f"in_{name}_dram"] = a
        args.append(nc.dram_tensor(f"in_{name}_dram", a.shape, mybir.dt.from_np(a.dtype), kind="ExternalInput").ap())
    out = nc.dram_tensor("out_0_dram", (1, T, D), F32, kind="ExternalOutput").ap()
    hybrid_layer(nc, *args, out)
    r = _run(nc, [arrays], core_ids=[0])
    return r.results[0]["out_0_dram"]
```

```python
import math
from contextlib import ExitStack

import numpy as np

import concourse.bass as bass
from concourse import mybir

ALU = mybir.AluOpType
ACT = mybir.ActivationFunctionType
AX = mybir.AxisListType
F32 = mybir.dt.float32
F32R = mybir.dt.float32r
I32 = mybir.dt.int32
U32 = mybir.dt.uint32

P = 128
D = 1024
KT = D // P
T = 512
NT = T // P
NQ, HD = 16, 64
WIN = 128
NBUCKET, MAXDIST = 32, 128
NE, GRP, EPG = 16, 4, 4
FF = 512
FT = FF // P
ALPHA = 2 ** 0.25
EPS = 1e-5
LRU_C = 8.0
MASKED = -1e30

COL_Q, COL_K, COL_V, COL_LX = 0, 1024, 1152, 1280
COL_LG, COL_GA, COL_GB = 2304, 3328, 4352
TILES = ([("k", 0, COL_K), ("v", 0, COL_V)]
         + [("lx", i, COL_LX + P * i) for i in range(KT)]
         + [("q", i, COL_Q + P * i) for i in range(KT)]
         + [("lg", i, COL_LG + P * i) for i in range(KT)]
         + [("gb", i, COL_GB + P * i) for i in range(KT)]
         + [("ga", i, COL_GA + P * i) for i in range(KT)])
NPROJ = len(TILES)
AT = {(kind, i): s for s, (kind, i, _) in enumerate(TILES)}
NSLOT = NPROJ + 1

SPLITS = ([[s + 2] for s in range(39)] + [[41, 42], [43, 44], [45, 46], [47, 48], [49]])

NU = 16
START = [13 + (3 * n) // 2 for n in range(NU)]
UNIT_AT = {s: n for n, s in enumerate(START)}

NOVER = 7
NBLK = NE + NOVER
TCOL = NBLK + 1
CH = 12
HLR = 6

C_ID, C_LOW, C_HOT, C_TOK, C_EXP, C_LT, C_GT, C_END = 0, 128, 256, 640, 644, 660, 676, 692
C_IOTA = C_END

FIRST, MORE, LAST, NUM = 0, NE, 2 * NE, 3 * NE


def constants():
    c = np.zeros((P, C_END + P), np.float32)
    c[:, C_ID:C_ID + P] = np.eye(P)
    c[:, C_LOW:C_LOW + P] = np.triu(np.ones((P, P)), 1)
    dist = 255 - np.arange(383)
    exact = NBUCKET // 2
    d = np.maximum(dist, 0)
    df = np.maximum(d, 1).astype(np.float32)
    large = exact + (np.log(df / exact) / math.log(MAXDIST / exact) * (NBUCKET - exact)).astype(np.int32)
    bucket = np.where(d < exact, d, np.minimum(large, NBUCKET - 1))
    for j in range(383):
        if 0 <= dist[j] < WIN:
            c[bucket[j], C_HOT + j] = 1.0
        else:
            c[NBUCKET, C_HOT + j] = MASKED
    c[NBUCKET, C_HOT + 383] = MASKED
    c[:, C_TOK:C_TOK + NT] = np.arange(P)[:, None] + P * np.arange(NT)[None]
    c[:, C_EXP:C_EXP + NE] = np.arange(NE)
    i, j = np.arange(4)[:, None], np.arange(4)[None]
    c[:, C_LT:C_LT + 16] = (i < j).astype(np.float32).ravel()
    c[:, C_GT:C_GT + 16] = (i > j).astype(np.float32).ravel()
    c[:, C_IOTA:C_IOTA + P] = np.arange(P)
    return c


def hybrid_layer(nc, x, c, ada_w, ada_b, w_in, attn_sink, rel_bias, conv_w, conv_b, lru_wa, lru_ba,
                 lru_wx, lru_bx, lru_lambda, w_out, ln1_g, ln1_b, router_w, router_b, moe_w_gate,
                 moe_w_up, moe_w_down, ln2_g, ln2_b, consts, out):
    def dram(name, shape, dt=F32):
        return nc.dram_tensor(name, shape, dt, kind="Internal").ap()

    bias_vec_d = dram("bias_vec_d", [NQ, 384])
    bias_rep_d = dram("bias_rep_d", [NQ, P, 384])
    mod_d = dram("mod_d", [32, P])
    u2_d = dram("u2_d", [T, D])
    y_d = dram("y_d", [(NBLK + 1) * P, D])

    ctx = ExitStack()
    with ctx:
        base = 16512
        top = [base]

        def region(nbytes):
            at = top[0]
            top[0] += nbytes
            assert top[0] <= 229344, top[0]
            return at

        def at(offset, name, shape, dt=F32):
            size = 4 * int(np.prod(shape[1:]))
            assert offset + size <= 229344, name
            return nc.alloc_sbuf_tensor_at(name, shape, dt, offset=offset), offset + size

        KB = 1024
        R_S = region(5 * KB + 768)
        R_A = region(16 * KB)
        R_B = region(16 * KB)
        R_W = region(36 * KB)
        R_Q = region(16 * KB)
        R_U = region(32 * KB)
        R_Y = region(16 * KB)
        R_Z = region(32 * KB)
        R_T = region(38 * KB)

        def small(name, shape, dt=F32):
            t, end = at(small.at, name, shape, dt)
            small.at = (end + 31) // 32 * 32
            assert small.at <= R_A
            return t
        small.at = R_S

        cst = small("cst", [P, C_END])
        ident = cst[:, C_ID:C_ID + P]
        ones = small("ones", [P, P])
        pcol = small("pcol", [P, 64])
        k8 = small("k8", [P, KT])
        nk8 = small("nk8", [P, KT])
        tiny = small("tiny", [P, 6, KT])
        ccol = small("ccol", [P, KT])
        cact = small("cact", [P, KT])
        mod1 = small("mod1", [P, 16])
        sinkp = small("sinkp", [P, NQ])
        mx = small("mx", [P, 4, 4])
        negm = small("negm", [P, 4, 4])
        sm = small("sm", [P, 4, 4])
        rsum = small("rsum", [P, 4, 4])
        rden = small("rden", [P, 4, 4])
        stats = small("stats", [P, 2, 6])
        aggr = small("aggr", [P, NT, 2])
        rstd = small("rstd", [P, NT])
        epst = small("epst", [P, 1])
        wA = small("wA", [P, NT])
        wB = small("wB", [P, NT])
        yrow = small("yrow", [P, 2, NT], U32)
        idn = small("idn", [P, 1], U32)

        x_sb, _ = at(R_A, "x_sb", [P, NT, D])
        uT, _ = at(R_B, "uT", [P, KT, T])
        uh, _ = at(R_U, "uh", [P, KT, T], F32R)
        ul, _ = at(R_U + 16 * KB, "ul", [P, KT, T], F32R)
        wax, _ = at(R_Q + 8 * KB, "wax", [P, 2, KT, P])
        assert R_U == R_Q + 16 * KB and R_Y == R_U + 32 * KB
        ada1, _ = at(R_Q, "ada1", [P, 8, 2 * D])
        raw = [at(R_W + 4 * KB * i, f"raw{i}", [P, 1024])[0] for i in range(3)]
        whi = [at(R_W + 12 * KB + 8 * KB * i, f"whi{i}", [P, KT, P], F32R)[0] for i in range(3)]
        wlo = [at(R_W + 16 * KB + 8 * KB * i, f"wlo{i}", [P, KT, P], F32R)[0] for i in range(3)]
        q_sb, _ = at(R_Q, "q_sb", [P, KT, T])
        yb, _ = at(R_Y, "yb", [P, KT, T])
        ix, _ = at(R_A, "ix", [P, KT, T])
        dec, _ = at(R_B, "dec", [P, KT, T])
        yh, _ = at(R_A, "yh", [P, KT, T], F32R)
        yl, _ = at(R_B, "yl", [P, KT, T], F32R)
        o = R_T
        ssb = []
        for i in range(2):
            t_, o = at(o, f"ssb{i}", [P, 2, 2, 256])
            ssb.append(t_)
        bias = []
        for i in range(2):
            t_, o = at(o, f"bias{i}", [P, 2, 2, 256])
            bias.append(t_)
        ptb, o = at(o, "ptb", [P, 2, 2, 2, P])
        onrm, o = at(o, "onrm", [P, 256])
        kk = []
        for i in range(2):
            t_, o = at(o, f"kk{i}", [P, T])
            kk.append(t_)
        vv, o = at(o, "vv", [P, NT, P])
        lru_at = o
        xpad, o = at(o, "xpad", [P, 520])
        xc = []
        for i in range(2):
            t_, o = at(o, f"xc{i}", [P, T])
            xc.append(t_)
        tt = []
        for i in range(2):
            t_, o = at(o, f"tt{i}", [P, T])
            tt.append(t_)
        assert o <= R_T + 38 * KB, o - R_T
        o = lru_at
        xg, gt = [], []
        for i in range(2):
            t_, o = at(o, f"xg{i}", [P, T])
            xg.append(t_)
            gt.append(at(R_T + 33 * KB + 2 * KB * i, f"gt{i}", [P, T])[0])
        assert o <= R_T + 33 * KB
        prm, o = at(R_T, "prm", [64, P])
        adab1, o = at(o, "adab1", [16, P])
        adab2 = small("adab2", [32, P])
        rbs, o = at(o, "rbs", [NBUCKET + 1, NQ])
        bvec, o = at(o, "bvec", [NQ, 384])
        sinkt, o = at(o, "sinkt", [P, NQ])
        ada2, _ = at(R_Z, "ada2", [P, 2, 2 * D])
        acc2, _ = at(R_Z + 16 * KB, "acc2", [P, 4 * D])
        mod2c, _ = at(R_Z, "mod2c", [P, 32])
        mod2r, _ = at(R_Z + KB, "mod2r", [32, P])
        woh, wol = [], []
        for k in range(KT):
            t_, o = at(R_Z + 8 * KB * k, f"woh{k}", [P, D], F32R)
            woh.append(t_)
            t_, _ = at(o, f"wol{k}", [P, D], F32R)
            wol.append(t_)
        rows = [at(R_W + 12 * KB + 4 * KB * i, f"row{i}", [P, D])[0] for i in range(6)]
        gate1r, g1r, b1r, a2r, b2r, zt = rows
        u2 = [at(R_W + 4 * KB * i, f"u2_{i}", [P, D])[0] for i in range(2)]
        u2T = [at(o_, f"u2T{i}", [P, KT, P])[0] for i, o_ in enumerate((R_W + 8 * KB, R_A + 12 * KB))]
        x1, _ = at(R_Q, "x1", [P, NT, D])
        def route(name, shape, dt=F32):
            t, route.at = at(route.at, name, shape, dt)
            route.at = (route.at + 31) // 32 * 32
            return t
        route.at = R_A
        rw = small("rw_sb", [P, KT, NE])
        rbr = small("rbr_sb", [1, NE])
        idx = route("idx", [P, TCOL], U32)
        ctrl = route("ctrl", [P, NUM + 1], I32)
        lg_ = route("lg_", [P, NT, NE])
        sc = route("sc", [P, NT, NE])
        cge = route("cge", [P, 256])
        cgt = route("cgt", [P, 256])
        rank = route("rank", [P, NT * GRP, EPG])
        sel = route("sel", [P, NT * GRP, EPG])
        gsc = route("gsc", [P, NT, GRP])
        grank = route("grank", [P, NT, GRP])
        mm = route("mm", [P, NT, NE])
        mpre = route("mpre", [P, NT, NE])
        mtot = route("mtot", [P, NE])
        pos = route("pos", [P, NT, NE])
        cnt = route("cnt", [P, NE])
        r2 = route("r2", [P, 2, NT, NE])
        t128 = route("t128", [P, 2, NT, NE])
        ovc = route("ovc", [P, NE])
        ovi = route("ovi", [P, NE])
        ovs = route("ovs", [P, NE])
        ctrlf = route("ctrlf", [P, NUM + 1])
        wr = route("wr", [P, 2, NT])
        wsum = route("wsum", [P, NT])
        pr = route("pr", [P, 2, NT])
        fr = route("fr", [P, 2, NT])
        wb = route("wb", [P, 2, NT])
        yrf = route("yrf", [P, 2, NT])
        red = route("red", [P, 2, NT])
        iota = route("iota", [P, P])
        at_pos = route("at_pos", [P, 2, NT, P], F32R)
        at_blk = route("at_blk", [P, 2, NT, TCOL], F32R)
        assert route.at <= R_A + 16 * KB, route.at - R_A
        mraw = [[at((R_U, R_B + 4 * KB)[par] + 4 * KB * i, f"mraw{par}_{i}", [P, 1024])[0] for i in range(CH)]
                for par in range(2)]
        mhi = [at(R_Z + 8 * KB * i, f"mhi{i}", [P, 2, 512], F32R)[0] for i in range(HLR)]
        mlo = [at(R_Z + 8 * KB * i + 4 * KB, f"mlo{i}", [P, 2, 512], F32R)[0] for i in range(HLR)]
        o = R_Z + 8 * KB * HLR
        xg_m, o = at(o, "xg_m", [P, D])
        xTh, o = at(o, "xTh", [P, KT, P], F32R)
        xTl, o = at(o, "xTl", [P, KT, P], F32R)
        h_sb, o = at(o, "h_sb", [P, FF])
        hTh, o = at(o, "hTh", [P, FT, P], F32R)
        hTl, o = at(o, "hTl", [P, FT, P], F32R)
        ysb, o = at(o, "ysb", [P, D])
        gate2r, _ = at(R_B, "gate2r", [P, D])
        g2r, _ = at(R_A + 8 * KB, "g2r", [P, D])
        be2r, _ = at(R_A + 12 * KB, "be2r", [P, D])
        fsum = small("fsum", [P, NT, 3])
        fin = [[at(R_U + 12 * KB * i + 4 * KB * j, f"fin{i}{j}", [P, D])[0] for j in range(3)] for i in range(NT)]

        psum = ctx.enter_context(nc.psum_tensor("psum", [P, 8, 512], F32))
        bank = [psum[:, i, :] for i in range(8)]
        scores = psum[:, 2:4, :].rearrange("p a (b s) -> p a b s", b=2)
        ptps = psum[:, 4:6, :].rearrange("p a (b h q) -> p a b h q", b=2, h=2)

        XB = (1, 2, 3, 5)

        def sem(name):
            return ctx.enter_context(nc.semaphore(name))

        const_in, param_in, x_in, small_in = (sem(n) for n in ("const_in", "param_in", "x_in", "small_in"))
        ada1_sem = [sem(f"ada1_in{j}") for j in range(8)]
        ada2_sem = [sem(f"ada2_in{j}") for j in range(2)]
        raw_in = [sem(f"raw_in{i}") for i in range(3)]
        mraw_in = [[sem(f"mraw_in{par}_{i}") for i in range(CH)] for par in range(2)]
        iota_in = sem("iota_in")
        bias_dma, bias_in0, bias_in1, kdup_in = sem("bias_dma"), sem("bias_in0"), sem("bias_in1"), sem("kdup_in")
        bias_in = [bias_in0, bias_in1]
        lruw_in, mod2_out, rows_in, x1_in = (sem(n) for n in ("lruw_in", "mod2_out", "rows_in", "x1_in"))
        u2_st = [sem(f"u2_st{i}") for i in range(2)]
        out_st = sem("out_st")
        fgather = [sem(f"fgather{i}") for i in range(NT)]
        names = """setup_done pcol_ps bvec_ps xT_ps u_even u_odd mod1_ps mod1_sb u_hi u_lo split_hi split_lo proj_ps evac
            pcol_sb exp_small dve_order pool_order c_done bvec_sb k_sb conv_done lr_ps li_ps er_done ti_done
            ix_done ta_done m2_done sqrt_done h_done sc_ps logit_done exp_done pt_ps pt_sb o_ps on_done
            ot_ps ya_done sq_done g_arg g_tanh gelu_done yb_done y_done y_hi y_lo ada2_used mod2_ps mod2_sb
            mod2_T mod2_row wout_ps ln_sqrt_in ln_sqrt xn_done x1_done u2_done u2T_ps u2T_sb logits_ps
            rt_exp_in rt_exp m_done pos_ps ctrl_done pool_went y_zero idx_ready onehots idx_ps
            fin_a fin_z fin_s fin_sqrt gath xT_m_ps xTh_m xTl_m chunk_used mhi_done mlo_done silu_done h_done_m
            ada1_sum hT_ps hTh_done hTl_done y_ev y_st fin_n fin_out xn_used z_done v_ps v_sb idn_done pool_in t_done""".split()
        S = {n: sem(n) for n in names}

        block = ctx.enter_context(nc.Block())
        w_in_v = w_in[0].rearrange("(k p) n -> p k n", p=P)
        ada_v = ada_w[0].rearrange("(p j) n -> p j n", j=8)
        wg_v = moe_w_gate[0].rearrange("e (c k p) f -> e c p k f", p=P, k=2)
        wu_v = moe_w_up[0].rearrange("e (c k p) f -> e c p k f", p=P, k=2)
        wd_v = moe_w_down[0].rearrange("e (c p) n -> e c p n", p=P)

        def chunk_src(e, ch):
            v = (wg_v, wu_v, wd_v)[ch // 4]
            return v[e, ch % 4]

        def load_chunk(sp, e, par, ch):
            dst = mraw[par][ch][:, :]
            sp.dma_start(dst.rearrange("p (k f) -> p k f", k=2) if ch < 8 else dst, chunk_src(e, ch))\
                .then_inc(mraw_in[par][ch], 16)

        @block.sync
        def _(sp):
            sp.dma_start(cst[:, :], consts[:, 0:C_END]).then_inc(const_in, 16)
            sp.dma_start(ccol[:, :], c[0].rearrange("(p j) -> p j", j=8)).then_inc(small_in, 16)
            sp.dma_start(adab1[:, :], ada_b[0, 0:2 * D].rearrange("(r p) -> r p", p=P)).then_inc(small_in, 16)
            for j, (a, b) in enumerate(((conv_w[0].rearrange("j (k p) -> (j k) p", p=P), 32),
                                        (conv_b[0].rearrange("(k p) -> k p", p=P), 8),
                                        (lru_ba[0].rearrange("(k p) -> k p", p=P), 8),
                                        (lru_bx[0].rearrange("(k p) -> k p", p=P), 8),
                                        (lru_lambda[0].rearrange("(k p) -> k p", p=P), 8))):
                r = (0, 32, 40, 48, 56)[j]
                sp.dma_start(prm[r:r + b, :], a).then_inc(param_in, 16)
            for j in range(8):
                sp.dma_start(ada1[:, j, :], ada_v[:, j, 0:2 * D]).then_inc(ada1_sem[j], 16)
            for t in range(NT):
                sp.dma_start(x_sb[:, t, :], x[0, t * P:(t + 1) * P, :]).then_inc(x_in, 16)

            def load_tile(t):
                if t >= 3:
                    sp.wait_ge(S["split_lo"], t - 2)
                if t < NPROJ:
                    col = TILES[t][2]
                    sp.dma_start(raw[t % 3][:, :].rearrange("p (k n) -> p k n", k=KT),
                                 w_in_v[:, :, col:col + P]).then_inc(raw_in[t % 3], 16)
                else:
                    k = t - NPROJ
                    sp.dma_start(raw[t % 3][:, :], w_out[0, k * P:(k + 1) * P, :]).then_inc(raw_in[t % 3], 16)

            for t in range(3):
                load_tile(t)
            sp.wait_ge(S["bvec_sb"], 1)
            sp.dma_start(bias_vec_d, bvec[:, :]).then_inc(bias_dma, 16)
            sp.wait_ge(bias_dma, 16)

            def replicate_bias(hg):
                src = bass.AP(bias_vec_d.tensor, 4 * hg * 384, [[384, 4], [0, P], [1, 384]])
                sp.dma_start(bias_rep_d[4 * hg:4 * hg + 4], src).then_inc(bias_dma, 16)

            def load_bias(hg):
                if hg >= 2:
                    sp.wait_ge(S["logit_done"], 4 * (hg - 1))
                for par in range(2):
                    src = bass.AP(bias_rep_d.tensor, (4 * hg + par) * P * 384 + 127,
                                  [[383, P], [2 * P * 384, 2], [1, 256]])
                    sp.dma_start(bias[hg % 2][:, par, :, :], src).then_inc(bias_in[hg % 2], 16)

            sp.wait_ge(S["mod1_ps"], 1)
            sp.dma_start(wax[:, 0, :, :], lru_wa[0].rearrange("h i j -> i h j")).then_inc(lruw_in, 16)
            sp.dma_start(wax[:, 1, :, :], lru_wx[0].rearrange("h i j -> i h j")).then_inc(lruw_in, 16)
            for t in range(3, NPROJ + KT):
                load_tile(t)
                if 5 <= t < 9:
                    replicate_bias(t - 5)
                if t == 6:
                    sp.wait_ge(S["k_sb"], 1)
                    sp.wait_ge(S["evac"], 1)
                    sp.dma_start(kk[0][64:128, :], kk[0][0:64, :]).then_inc(kdup_in, 16)
                    sp.dma_start(kk[1][0:64, :], kk[1][64:128, :]).then_inc(kdup_in, 16)
                if t == 10:
                    sp.wait_ge(bias_dma, 5 * 16)
                    load_bias(0)
                    load_bias(1)
                if t == START[8] - 1:
                    load_bias(2)
                if t == START[12] - 1:
                    load_bias(3)
                if t == 36:
                    sp.wait_ge(S["mod2_row"], 1)
                    sp.dma_start(mod_d, mod2r[:, :]).then_inc(mod2_out, 16)
                    sp.wait_ge(mod2_out, 16)
            sp.wait_ge(S["proj_ps"], NPROJ)
            mod_flat = mod_d.rearrange("a b -> (a b)")

            def row_of(i):
                return mod_flat[i * D:(i + 1) * D].partition_broadcast(P)
            sp.dma_start(gate1r[:, :], row_of(0)).then_inc(rows_in, 16)
            sp.dma_start(g1r[:, :], ln1_g[0].partition_broadcast(P)).then_inc(rows_in, 16)
            sp.dma_start(b1r[:, :], ln1_b[0].partition_broadcast(P)).then_inc(rows_in, 16)
            sp.dma_start(b2r[:, :], row_of(1)).then_inc(rows_in, 16)
            sp.dma_start(a2r[:, :], row_of(2)).then_inc(rows_in, 16)
            sp.wait_ge(S["y_lo"], KT)
            for t in range(NT):
                sp.dma_start(x1[:, t, :], x[0, t * P:(t + 1) * P, :]).then_inc(x1_in, 16)
            for ch in range(CH):
                load_chunk(sp, 0, 0, ch)
            for t in range(NT):
                sp.wait_ge(S["u2_done"], t + 1)
                sp.dma_start(u2_d[t * P:(t + 1) * P, :], u2[t % 2][:, :]).then_inc(u2_st[t % 2], 16)
            sp.wait_ge(S["wout_ps"], 2 * NT)
            sp.dma_start(iota[:, :], consts[:, C_IOTA:C_IOTA + P]).then_inc(iota_in, 16)
            sp.dma_start(gate2r[:, :], row_of(3)).then_inc(rows_in, 16)
            for ch in range(3):
                load_chunk(sp, 1, 1, ch)
            sp.wait_ge(S["x1_done"], NT)
            for ch in range(6, CH):
                load_chunk(sp, 1, 1, ch)
            for q in u2_st:
                sp.wait_ge(q, 16 * NT // 2)
            sp.wait_ge(S["logits_ps"], NT)
            for ch in range(3, 6):
                load_chunk(sp, 1, 1, ch)
            sp.wait_ge(S["ctrl_done"], 1)
            sp.wait_ge(S["idx_ps"], 1)
            sp.dma_start(g2r[:, :], ln2_g[0].partition_broadcast(P)).then_inc(rows_in, 16)
            sp.dma_start(be2r[:, :], ln2_b[0].partition_broadcast(P)).then_inc(rows_in, 16)
            with sp.Fori(1, NE // 2) as pair:
                for par in range(2):
                    last = sp.value_load(ctrl[0:1, bass.ds(2 * pair + (LAST + par - 2), 1)], min_val=0, max_val=NBLK - 1)
                    for ch in range(CH):
                        sp.wait_ge(S["mlo_done"], last * CH + (ch + 1))
                        load_chunk(sp, 2 * pair + par, par, ch)
            for t in range(NT):
                sp.wait_ge(S["fin_out"], t + 1)
                sp.dma_start(out[0, t * P:(t + 1) * P, :], fin[t][0][:, :]).then_inc(out_st, 16)
            sp.wait_ge(out_st, 16 * NT)

        @block.gpsimd
        def _(pool):
            pool.dma_start(rbs[0:NBUCKET, :], rel_bias).then_inc(S["pool_in"], 16)
            pool.dma_start(sinkt[:, :], attn_sink[0].partition_broadcast(P)).then_inc(S["pool_in"], 16)
            pool.dma_start(adab2[:, :], ada_b[0, 2 * D:6 * D].rearrange("(r p) -> r p", p=P)).then_inc(S["pool_in"], 16)
            pool.dma_start(rw[:, :, :], router_w.rearrange("(k p) e -> p k e", p=P)).then_inc(S["pool_in"], 16)
            pool.dma_start(rbr[:, :], router_b.rearrange("(a e) -> a e", a=1)).then_inc(S["pool_in"], 16)
            pool.wait_ge(S["u_lo"], 1)
            def load_ada2(n):
                half = n % 2
                pool.dma_start(ada2[:, half, :],
                               ada_v[:, n // 2, (2 + 2 * half) * D:(4 + 2 * half) * D]).then_inc(ada2_sem[half], 16)

            load_ada2(0)
            load_ada2(1)
            for n in range(16):
                j, half = n // 2, n % 2
                part = acc2[:, half * 2 * D:(half + 1) * 2 * D]
                pool.wait_ge(ada2_sem[half], 16 * (j + 1))
                if j == 0:
                    pool.tensor_scalar(part, ada2[:, half, :], cact[:, 0:1], None, ALU.mult).then_inc(S["ada2_used"], 1)
                else:
                    pool.tensor_scalar(ada2[:, half, :], ada2[:, half, :], cact[:, j:j + 1], None,
                                       ALU.mult).then_inc(S["pool_order"], 1)
                    pool.wait_ge(S["pool_order"], n - 1)
                    pool.wait_ge(S["ada2_used"], n)
                    pool.tensor_tensor(part, part, ada2[:, half, :], ALU.add).then_inc(S["ada2_used"], 1)
                if n + 2 < 16:
                    pool.wait_ge(S["ada2_used"], n + 1)
                    load_ada2(n + 2)
            pool.wait_ge(S["ada2_used"], 16)
            pool.memset(ada2[:, 0, 0:D], 0.0).then_inc(S["z_done"], 1)
            pool.wait_ge(S["z_done"], 1)
            for b in range(NE + 1, NBLK + 1):
                pool.dma_start(y_d[b * P:(b + 1) * P, :], ada2[:, 0, 0:D]).then_inc(S["y_zero"], 16)
            pool.dma_start(y_d[0:P, :], ada2[:, 1, 0:D]).then_inc(S["y_st"], 16)
            pool.wait_ge(S["y_zero"], 16 * NOVER)
            for t in range(NT):
                pool.wait_ge(S["xn_done"], t + 1)
                pool.tensor_tensor(x1[:, t, :], zt[:, :], g1r[:, :], ALU.mult).then_inc(S["xn_used"], 1)
                pool.wait_ge(S["xn_used"], t + 1)
                pool.tensor_tensor(x1[:, t, :], x1[:, t, :], b1r[:, :], ALU.add).then_inc(S["x1_done"], 1)
            for q in u2_st:
                pool.wait_ge(q, 16 * NT // 2)
            pool.wait_ge(S["idx_ready"], 1)
            pool.indirect_dma_start(xg_m[:, :], None, u2_d,
                                    bass.IndirectOffsetOnAxis(ap=idx[:, 0:1], axis=0)).then_inc(S["gath"], 16)
            pool.wait_ge(S["ctrl_done"], 1)
            nblk = pool.value_load(ctrl[0:1, NUM:NUM + 1], min_val=NE, max_val=NBLK)

            def store_rows(b):
                pool.wait_ge(S["y_ev"], b * 2 + 2)
                pool.sem_inc(S["pool_went"], 1)
                pool.dma_start(y_d[bass.ds(b * P, P), :], ysb[:, :]).then_inc(S["y_st"], 16)

            with pool.Fori(0, nblk) as b:
                pool.wait_ge(S["xT_m_ps"], b + 1)
                pool.tensor_copy(idn[:, :], idx[:, bass.ds(b + 1, 1)]).then_inc(S["idn_done"], 1)
                pool.wait_ge(S["idn_done"], b + 1)
                pool.sem_inc(S["pool_went"], 1)
                pool.indirect_dma_start(xg_m[:, :], None, u2_d,
                                        bass.IndirectOffsetOnAxis(ap=idn[:, 0:1], axis=0)).then_inc(S["gath"], 16)
                store_rows(b)
            store_rows(nblk)
            pool.wait_ge(S["y_st"], nblk * 16 + 32)
            pool.sem_inc(S["pool_went"], 1)
            pool.wait_ge(S["x1_done"], NT)
            for t in range(NT):
                for r in range(2):
                    pool.indirect_dma_start(fin[t][1 + r][:, :], None, y_d,
                                            bass.IndirectOffsetOnAxis(ap=yrow[:, r, t:t + 1], axis=0)).then_inc(fgather[t], 16)

        @block.scalar
        def _(act):
            A = act.activation

            act.wait_ge(small_in, 32)
            A(tiny[:, 0, :], ccol[:, :], ACT.Exp, scale=-1.0).then_inc(S["exp_small"], 1)
            act.wait_ge(S["pcol_ps"], 1)
            A(pcol[:, :], bank[7][:, 0:64], ACT.Copy).then_inc(S["pcol_sb"], 1)
            act.wait_ge(S["dve_order"], 2)
            A(tiny[:, 1, :], tiny[:, 1, :], ACT.Exp).then_inc(S["exp_small"], 1)
            act.wait_ge(S["bvec_ps"], 1)
            A(bvec[:, :], psum[0:16, 6, 0:384], ACT.Copy).then_inc(S["bvec_sb"], 1)

            def split(t):
                act.wait_ge(raw_in[t % 3], 16 * (t // 3 + 1))
                if t < NPROJ:
                    if t >= 3:
                        act.wait_ge(S["proj_ps"], t - 2)
                        act.wait_ge(S["split_lo"], t - 2)
                    A(whi[t % 3][:, :, :], raw[t % 3][:, :].rearrange("p (k n) -> p k n", k=KT), ACT.Copy)\
                        .then_inc(S["split_hi"], 1)
                else:
                    k = t - NPROJ
                    act.wait_ge(S["mod2_row"], 1)
                    act.wait_ge(mod2_out, 16)
                    act.wait_ge(S["y_zero"], 16 * NOVER)
                    act.wait_ge(S["y_st"], 16)
                    if k >= 4:
                        act.wait_ge(S["ot_ps"], NU)
                        act.wait_ge(S["gelu_done"], KT)
                    A(woh[k][:, :], raw[t % 3][:, :], ACT.Copy).then_inc(S["split_hi"], 1)

            act.wait_ge(S["mod1_sb"], 2)
            for k in range(KT):
                bias_, scale_ = mod1[:, k:k + 1], mod1[:, 8 + k:9 + k]
                if k % 2 == 1:
                    act.wait_ge(S["u_odd"], k // 2 + 1)
                    A(uh[:, k, :], uT[:, k, :], ACT.Copy).then_inc(S["u_hi"], 1)
                else:
                    act.wait_ge(S["xT_ps"], k + 1)
                    A(uh[:, k, :], bank[XB[k % 4]], ACT.Identity, bias=bias_, scale=scale_).then_inc(S["u_hi"], 1)
                    A(uT[:, k, :], bank[XB[k % 4]], ACT.Identity, bias=bias_, scale=scale_).then_inc(S["u_even"], 1)
                if k == 1:
                    split(0)
            split(1)

            def evacuate(s):
                kind, i, _ = TILES[s]
                b = bank[s % 2]
                act.wait_ge(S["proj_ps"], s + 1)
                if kind == "k":
                    A(kk[0][0:64, :], psum[0:64, s % 2, :], ACT.Copy).then_inc(S["k_sb"], 1)
                    A(kk[1][64:128, :], psum[64:128, s % 2, :], ACT.Copy).then_inc(S["evac"], 1)
                elif kind == "v":
                    A(tt[0][:, :], b, ACT.Copy).then_inc(S["evac"], 1)
                elif kind == "lx":
                    if i >= 1:
                        act.wait_ge(S["conv_done"], i)
                    A(xpad[:, 3:3 + T], b, ACT.Copy).then_inc(S["evac"], 1)
                elif kind == "q":
                    A(q_sb[:, i, :], b, ACT.Copy, scale=HD ** -0.5).then_inc(S["evac"], 1)
                elif kind == "lg":
                    if i >= 2:
                        act.wait_ge(S["gelu_done"], i - 1)
                    A(gt[i % 2][:, :], b, ACT.Square).then_inc(S["sq_done"], 1)
                    A(xg[i % 2][:, :], b, ACT.Copy).then_inc(S["evac"], 1)
                elif kind == "gb":
                    act.wait_ge(S["gelu_done"], min(KT, KT - 1 + i))
                    if i >= 2:
                        act.wait_ge(S["yb_done"], i - 1)
                    A(gt[i % 2][:, :], b, ACT.Tanh, scale=0.5).then_inc(S["evac"], 1)
                else:
                    act.wait_ge(S["yb_done"], min(KT, KT - 1 + i))
                    if i >= 2:
                        act.wait_ge(S["y_done"], i - 1)
                    A(gt[i % 2][:, :], b, ACT.Tanh, scale=0.5).then_inc(S["evac"], 1)

            for s in range(NPROJ + 2):
                if 1 <= s <= NPROJ:
                    evacuate(s - 1)
                n = UNIT_AT.get(s - 3)
                if n is not None:
                    act.wait_ge(S["pt_ps"], n + 1)
                    if n >= 1:
                        act.wait_ge(S["o_ps"], n)
                    if n % 4 == 0:
                        A(ptb[:, :, :, 1, :], ptps[:, :, :, 1, :], ACT.Copy).then_inc(S["pt_sb"], 1)
                    else:
                        A(ptb[:, :, :, :, :], ptps[:, :, :, :, :], ACT.Copy).then_inc(S["pt_sb"], 1)
                i = s - 5
                if 0 <= i < KT:
                    act.wait_ge(S["lr_ps"], i + 1)
                    A(dec[:, i, :], bank[6], ACT.Sigmoid, bias=pcol[:, 40 + i:41 + i]).then_inc(S["er_done"], 1)
                for t in SPLITS[s]:
                    split(t)
                i = s - 5
                if 0 <= i < KT:
                    act.wait_ge(S["li_ps"], i + 1)
                    A(ix[:, i, :], bank[7], ACT.Sigmoid, bias=pcol[:, 48 + i:49 + i]).then_inc(S["ti_done"], 1)
                    act.wait_ge(S["er_done"], i + 1)
                    A(yb[:, i, :], dec[:, i, :], ACT.Tanh, scale=k8[:, i:i + 1]).then_inc(S["t_done"], 1)
                if s == 13:
                    act.wait_ge(S["t_done"], KT)
                    for i in range(KT):
                        A(dec[:, i, :], dec[:, i, :], ACT.Exp, scale=nk8[:, i:i + 1]).then_inc(S["ta_done"], 1)
                if s == 17:
                    act.wait_ge(S["m2_done"], KT)
                    A(yb[:, :, :], yb[:, :, :], ACT.Sqrt).then_inc(S["sqrt_done"], 1)
                if s == 4:
                    act.wait_ge(S["v_ps"], 1)
                    A(vv[:, :, :], bank[5].rearrange("p (t n) -> p t n", t=NT), ACT.Copy).then_inc(S["v_sb"], 1)
                n = UNIT_AT.get(s - 5)
                if n is not None:
                    hg, blk_ = n // 4, n % 4
                    act.wait_ge(S["ot_ps"], n + 1)
                    A(q_sb[:, 2 * hg:2 * hg + 2, blk_ * P:(blk_ + 1) * P],
                      bank[7][:, 0:256].rearrange("p (i q) -> p i q", i=2), ACT.Copy).then_inc(S["ya_done"], 1)
                i = s - (AT["lg", 0] + 1)
                if 0 <= i < KT:
                    act.wait_ge(S["g_arg"], i + 1)
                    A(gt[i % 2][:, :], gt[i % 2][:, :], ACT.Tanh, scale=math.sqrt(2 / math.pi)).then_inc(S["g_tanh"], 1)
                n = UNIT_AT.get(s - 1)
                if n is not None:
                    act.wait_ge(S["logit_done"], n + 1)
                    lo = P if n % 4 == 0 else 0
                    for a in range(2):
                        for b in range(2):
                            v = ssb[n % 2][:, a, b, lo:256]
                            A(v, v, ACT.Exp, bias=negm[:, n % 4, 2 * a + b:2 * a + b + 1],
                              accum_out=rsum[:, n % 4, 2 * a + b:2 * a + b + 1]).then_inc(S["exp_done"], 1)
                    A(sm[:, n % 4, :], sm[:, n % 4, :], ACT.Exp).then_inc(S["exp_done"], 1)
                i = s - (AT["ga", 0] + 2)
                if 0 <= i < KT:
                    act.wait_ge(S["y_done"], i + 1)
                    A(yh[:, i, :], q_sb[:, i, :], ACT.Copy).then_inc(S["y_hi"], 1)
            def ln_sqrt(t):
                act.wait_ge(S["ln_sqrt_in"], t + 1)
                A(rstd[:, t:t + 1], aggr[:, t, 1:2], ACT.Sqrt, bias=epst[:, 0:1]).then_inc(S["ln_sqrt"], 1)

            ln_sqrt(0)
            ln_sqrt(1)
            for t in range(NT):
                act.wait_ge(S["u2T_ps"], t + 1)
                if t == 1:
                    act.wait_ge(S["wout_ps"], 2 * NT)
                if t >= 2:
                    act.wait_ge(S["logits_ps"], t - 1)
                b0 = 4 * (1 - t % 2)
                A(u2T[t % 2][:, :, :], psum[:, b0:b0 + 2, :].rearrange("p a (k n) -> p (a k) n", k=4), ACT.Copy)\
                    .then_inc(S["u2T_sb"], 1)
                if t + 2 < NT:
                    ln_sqrt(t + 2)
            act.wait_ge(S["rt_exp_in"], 1)
            A(sc[:, :, :], lg_[:, :, :], ACT.Exp).then_inc(S["rt_exp"], 1)

            def hi(b, par, ch):
                act.wait_ge(S["chunk_used"], b * CH + (ch + 1))
                A(mhi[ch % HLR][:, :, :], mraw[par][ch][:, :].rearrange("p (k f) -> p k f", k=2), ACT.Copy)\
                    .then_inc(S["mhi_done"], 1)

            def x_hi(b):
                act.wait_ge(S["xT_m_ps"], b + 1)
                for a in range(2):
                    A(xTh[:, 4 * a:4 * a + 4, :], psum[:, 2 + a, :].rearrange("p (k n) -> p k n", k=4), ACT.Copy)\
                        .then_inc(S["xTh_m"], 1)

            def y_out(b):
                act.wait_ge(S["chunk_used"], b * CH + HLR)
                act.wait_ge(S["y_st"], b * 16 + 16)
                for a in range(2):
                    A(ysb[:, a * 512:(a + 1) * 512], bank[5 + a], ACT.Copy).then_inc(S["y_ev"], 1)

            def act_block(b, par, pair=None):
                for ch in range(CH):
                    if pair is not None:
                        act.wait_ge(mraw_in[par][ch], pair * 16 + 16)
                    hi(b, par, ch)
                    if ch == 5:
                        y_out(b)
                    if ch == 9:
                        A(h_sb[:, :], bank[0], ACT.Silu).then_inc(S["silu_done"], 1)
                for a in range(2):
                    act.wait_ge(S["hT_ps"], b * 2 + (a + 1))
                    A(hTh[:, 2 * a:2 * a + 2, :], bank[4 + 3 * a][:, 0:256].rearrange("p (k n) -> p k n", k=2),
                      ACT.Copy).then_inc(S["hTh_done"], 1)
                x_hi(b + 1)

            act.wait_ge(S["rt_exp"], 1)
            A(tiny[:, 0, :], tiny[:, 0, :], ACT.Silu).then_inc(S["rt_exp"], 1)
            x_hi(0)
            act.wait_ge(S["wout_ps"], 2 * NT)
            act.wait_ge(S["ctrl_done"], 1)
            with act.Fori(0, NE // 2) as pair:
                for par in range(2):
                    first = act.value_load(ctrl[0:1, bass.ds(2 * pair + (FIRST + par), 1)], min_val=0, max_val=NBLK - 1)
                    more = act.value_load(ctrl[0:1, bass.ds(2 * pair + (MORE + par), 1)], min_val=0, max_val=3)
                    act_block(first, par, pair)
                    with act.If(more > 0):
                        with act.Fori(0, more) as j:
                            act_block(first + 1 + j, par)
            nblk = act.value_load(ctrl[0:1, NUM:NUM + 1], min_val=NE, max_val=NBLK)
            y_out(nblk)
            def weigh(t):
                act.wait_ge(fgather[t], 32)
                A(fin[t][1][:, :], fin[t][1][:, :], ACT.Copy, scale=wA[:, t:t + 1]).then_inc(S["fin_a"], 1)

            def moments(t):
                z, spare = fin[t][0][:, :], fin[t][1][:, :]
                act.wait_ge(S["fin_z"], t + 1)
                A(spare, z, ACT.Copy, accum_out=fsum[:, t, 0:1]).then_inc(S["fin_s"], 1)
                act.wait_ge(S["fin_s"], 3 * t + 1)
                A(fsum[:, t, 1:2], fsum[:, t, 0:1], ACT.Copy, scale=-1.0 / D).then_inc(S["fin_s"], 1)
                act.wait_ge(S["fin_s"], 3 * t + 2)
                A(spare, z, ACT.Square, bias=fsum[:, t, 1:2], accum_out=fsum[:, t, 2:3]).then_inc(S["fin_s"], 1)
                act.wait_ge(S["fin_s"], 3 * t + 3)
                A(rstd[:, t:t + 1], fsum[:, t, 2:3], ACT.Sqrt, bias=epst[:, 0:1], scale=1.0 / D).then_inc(S["fin_sqrt"], 1)

            weigh(0)
            for t in range(NT):
                if t + 1 < NT:
                    weigh(t + 1)
                moments(t)

        @block.vector
        def _(dve):
            V = nc.vector
            n_order = [0]

            def mark(ins):
                n_order[0] += 1
                ins.then_inc(S["dve_order"], 1)
                return n_order[0]

            def chain(ins):
                dve.wait_ge(S["dve_order"], mark(ins))

            dve.sem_inc(S["h_done_m"], 2)
            V.memset(ones[:, :], 1.0).then_inc(S["setup_done"], 1)
            V.memset(rbs[NBUCKET:NBUCKET + 1, :], 1.0).then_inc(S["setup_done"], 1)
            V.memset(xpad[:, 0:3], 0.0).then_inc(S["setup_done"], 1)
            V.memset(epst[:, :], EPS).then_inc(S["setup_done"], 1)
            dve.wait_ge(S["pcol_sb"], 1)
            lam = pcol[:, 56:64]
            chain(V.tensor_scalar(tiny[:, 2, :], lam, -1.0, None, ALU.mult))
            chain(V.tensor_tensor(tiny[:, 1, :], tiny[:, 2, :], lam, ALU.min))
            dve.wait_ge(S["exp_small"], 1)
            chain(V.tensor_scalar(tiny[:, 0, :], tiny[:, 0, :], 1.0, None, ALU.add))
            chain(V.reciprocal(tiny[:, 0, :], tiny[:, 0, :]))
            V.tensor_tensor(cact[:, :], ccol[:, :], tiny[:, 0, :], ALU.mult).then_inc(S["c_done"], 1)
            dve.wait_ge(S["c_done"], 1)
            for j in range(8):
                dve.wait_ge(ada1_sem[j], 16)
                if j == 0:
                    V.tensor_scalar(ada1[:, 0, :], ada1[:, 0, :], cact[:, 0:1], None, ALU.mult)\
                        .then_inc(S["ada1_sum"], 1)
                else:
                    dve.wait_ge(S["ada1_sum"], j)
                    V.scalar_tensor_tensor(ada1[:, 0, :], ada1[:, j, :], cact[:, j:j + 1], ada1[:, 0, :],
                                           ALU.mult, ALU.add).then_inc(S["ada1_sum"], 1)
            def split(t):
                dve.wait_ge(S["split_hi"], t + 1)
                if t < NPROJ:
                    r3 = raw[t % 3][:, :].rearrange("p (k n) -> p k n", k=KT)
                    V.tensor_tensor(wlo[t % 3][:, :, :], r3, whi[t % 3][:, :, :].bitcast(F32), ALU.subtract)\
                        .then_inc(S["split_lo"], 1)
                else:
                    k = t - NPROJ
                    V.tensor_tensor(wol[k][:, :], raw[t % 3][:, :], woh[k][:, :].bitcast(F32), ALU.subtract)\
                        .then_inc(S["split_lo"], 1)

            dve.wait_ge(S["mod1_ps"], 1)
            V.tensor_copy(mod1[:, 0:8], bank[4][:, 0:8]).then_inc(S["mod1_sb"], 1)
            V.tensor_scalar(mod1[:, 8:16], bank[4][:, 8:16], 1.0, None, ALU.add).then_inc(S["mod1_sb"], 1)
            dve.wait_ge(S["mod1_sb"], 2)

            def u_low(k):
                dve.wait_ge(S["u_hi"], k + 1)
                if k % 2 == 0:
                    dve.wait_ge(S["u_even"], k // 2 + 1)
                else:
                    dve.wait_ge(S["u_odd"], k // 2 + 1)
                V.tensor_tensor(ul[:, k, :], uT[:, k, :], uh[:, k, :].bitcast(F32), ALU.subtract).then_inc(S["u_lo"], 1)

            for k in range(0, KT, 2):
                dve.wait_ge(S["xT_ps"], k + 2)
                V.tensor_scalar(uT[:, k + 1, :], bank[XB[(k + 1) % 4]], mod1[:, 9 + k:10 + k], mod1[:, k + 1:k + 2],
                                ALU.mult, ALU.add).then_inc(S["u_odd"], 1)
                u_low(k)
                u_low(k + 1)
                if k == 0:
                    split(0)
            split(1)
            dve.wait_ge(S["u_lo"], KT)
            dve.wait_ge(S["exp_small"], 2)
            chain(V.tensor_scalar(tiny[:, 3, :], tiny[:, 1, :], 2.0, None, ALU.add))
            chain(V.reciprocal(tiny[:, 3, :], tiny[:, 3, :]))
            chain(V.tensor_tensor(tiny[:, 3, :], tiny[:, 3, :], tiny[:, 1, :], ALU.mult))
            chain(V.tensor_tensor(tiny[:, 4, :], tiny[:, 3, :], tiny[:, 3, :], ALU.mult))
            chain(V.tensor_scalar(tiny[:, 5, :], tiny[:, 4, :], 1.0 / 19, 1.0 / 17, ALU.mult, ALU.add))
            for m in (15, 13, 11, 9, 7, 5, 3, 1):
                chain(V.tensor_tensor(tiny[:, 5, :], tiny[:, 5, :], tiny[:, 4, :], ALU.mult))
                chain(V.tensor_scalar(tiny[:, 5, :], tiny[:, 5, :], 1.0 / m, None, ALU.add))
            chain(V.scalar_tensor_tensor(tiny[:, 5, :], tiny[:, 5, :], 2.0, tiny[:, 3, :], ALU.mult, ALU.mult))
            chain(V.scalar_tensor_tensor(tiny[:, 5, :], tiny[:, 2, :], 0.0, tiny[:, 5, :], ALU.max, ALU.add))
            mark(V.tensor_scalar(k8[:, :], tiny[:, 5, :], LRU_C, None, ALU.mult))
            mark(V.tensor_scalar(nk8[:, :], tiny[:, 5, :], -LRU_C, None, ALU.mult))
            dve.wait_ge(S["setup_done"], 4)
            dve.wait_ge(S["pool_in"], 16 * 5)
            chain(V.tensor_copy(sinkp[:, :].rearrange("p (g a b) -> p g a b", g=4, a=2),
                                sinkt[:, :].rearrange("p (g b a) -> p g a b", g=4, a=2)))

            for s in range(NPROJ + 2):
                n = UNIT_AT.get(s - 4)
                if n is not None:
                    r = n % 4
                    dve.wait_ge(S["exp_done"], 5 * (n + 1))
                    chain(V.tensor_tensor(rden[:, r, :], rsum[:, r, :], sm[:, r, :], ALU.add))
                    chain(V.reciprocal(rden[:, r, :], rden[:, r, :]))
                    dve.wait_ge(S["o_ps"], n + 1)
                    if n >= 1:
                        dve.wait_ge(S["ot_ps"], n)
                    for b in range(2):
                        ins = V.tensor_tensor(
                            onrm[:, b * P:(b + 1) * P].rearrange("p (a d) -> p a d", a=2),
                            bank[6][:, b * P:(b + 1) * P].rearrange("p (a d) -> p a d", a=2),
                            rden[:, r, b:4:2].unsqueeze(2).to_broadcast([P, 2, HD]), ALU.mult)
                        if b == 0:
                            mark(ins)
                        else:
                            ins.then_inc(S["on_done"], 1)
                n = UNIT_AT.get(s - 1)
                if n is not None:
                    hg, first = n // 4, n % 4 == 0
                    lo = P if first else 0
                    r, sl = n % 4, ssb[n % 2][:, :, :, lo:256]
                    dve.wait_ge(S["sc_ps"], n + 1)
                    dve.wait_ge(bias_in[hg % 2], 32 * (hg // 2 + 1))
                    if n >= 2:
                        dve.wait_ge(S["pt_ps"], n - 1)
                    for a in range(2):
                        k_ = mark(V.tensor_tensor(ssb[n % 2][:, a, :, lo:256], scores[:, a, :, lo:256],
                                                  bias[hg % 2][:, a, :, lo:256], ALU.add))
                    dve.wait_ge(S["dve_order"], k_)
                    chain(V.tensor_reduce(mx[:, r, :].rearrange("p (a b) -> p a b", a=2), sl, AX.X, ALU.max))
                    chain(V.tensor_tensor(mx[:, r, :], mx[:, r, :], sinkp[:, 4 * hg:4 * hg + 4], ALU.max))
                    if n >= 4:
                        dve.wait_ge(S["on_done"], n - 3)
                    k_ = mark(V.tensor_scalar(negm[:, r, :], mx[:, r, :], -1.0, None, ALU.mult))
                    dve.wait_ge(S["dve_order"], k_)
                    V.tensor_tensor(sm[:, r, :], sinkp[:, 4 * hg:4 * hg + 4], mx[:, r, :], ALU.subtract)\
                        .then_inc(S["logit_done"], 1)
                for t in SPLITS[s]:
                    split(t)
                i = s - 5
                if 0 <= i < KT:
                    dve.wait_ge(S["ti_done"], i + 1)
                    V.tensor_tensor(ix[:, i, :], ix[:, i, :], xc[i % 2][:, :], ALU.mult).then_inc(S["ix_done"], 1)
                i = s - 3
                if 0 <= i < KT:
                    dve.wait_ge(S["evac"], AT["lx", i] + 1)
                    v = xc[i % 2]
                    if i >= 2:
                        dve.wait_ge(S["li_ps"], i - 1)
                        dve.wait_ge(S["ix_done"], i - 1)
                    chain(V.tensor_scalar(v[:, :], xpad[:, 0:T], pcol[:, i:i + 1], pcol[:, 32 + i:33 + i],
                                          ALU.mult, ALU.add))
                    for j in range(1, 4):
                        ins = V.scalar_tensor_tensor(v[:, :], xpad[:, j:j + T], pcol[:, 8 * j + i:8 * j + i + 1],
                                                     v[:, :], ALU.mult, ALU.add)
                        if j < 3:
                            chain(ins)
                        else:
                            ins.then_inc(S["conv_done"], 1)
                if 14 <= s <= 16:
                    for i in ((0, 1), (2, 3, 4), (5, 6, 7))[s - 14]:
                        dve.wait_ge(S["ta_done"], i + 1)
                        k_ = mark(V.tensor_tensor(tt[i % 2][:, :], dec[:, i, :], dec[:, i, :], ALU.mult))
                        dve.wait_ge(S["dve_order"], k_)
                        V.scalar_tensor_tensor(yb[:, i, :], tt[i % 2][:, :], 1.0, yb[:, i, :], ALU.add, ALU.mult)\
                            .then_inc(S["m2_done"], 1)
                i = s - 18
                if 0 <= i < KT:
                    dve.wait_ge(S["sqrt_done"], 1)
                    dve.wait_ge(S["ix_done"], i + 1)
                    chain(V.scalar_tensor_tensor(ix[:, i, :], ix[:, i, :], 1.0, yb[:, i, :], ALU.mult, ALU.mult))
                    V.tensor_tensor_scan(yb[:, i, :], dec[:, i, :], ix[:, i, :], 0.0, ALU.mult, ALU.add)\
                        .then_inc(S["h_done"], 1)
                i = s - (AT["lg", 0] + 1)
                if 0 <= i < KT:
                    dve.wait_ge(S["sq_done"], i + 1)
                    chain(V.tensor_scalar(gt[i % 2][:, :], gt[i % 2][:, :], 0.044715, 1.0, ALU.mult, ALU.add))
                    dve.wait_ge(S["evac"], AT["lg", i] + 1)
                    V.tensor_tensor(gt[i % 2][:, :], gt[i % 2][:, :], xg[i % 2][:, :], ALU.mult).then_inc(S["g_arg"], 1)
                i = s - (AT["lg", 0] + 2)
                if 0 <= i < KT:
                    dve.wait_ge(S["g_tanh"], i + 1)
                    dve.wait_ge(S["h_done"], i + 1)
                    chain(V.scalar_tensor_tensor(gt[i % 2][:, :], gt[i % 2][:, :], 1.0, xg[i % 2][:, :], ALU.add, ALU.mult))
                    V.scalar_tensor_tensor(yb[:, i, :], gt[i % 2][:, :], 0.5, yb[:, i, :], ALU.mult, ALU.mult)\
                        .then_inc(S["gelu_done"], 1)
                i = s - (AT["gb", 0] + 1)
                if 0 <= i < KT:
                    dve.wait_ge(S["evac"], AT["gb", i] + 1)
                    dve.wait_ge(S["gelu_done"], i + 1)
                    V.scalar_tensor_tensor(yb[:, i, :], gt[i % 2][:, :], 1.0, yb[:, i, :], ALU.add, ALU.mult)\
                        .then_inc(S["yb_done"], 1)
                i = s - (AT["ga", 0] + 1)
                if 0 <= i < KT:
                    dve.wait_ge(S["evac"], AT["ga", i] + 1)
                    dve.wait_ge(S["ya_done"], 4 * (i // 2 + 1))
                    dve.wait_ge(S["yb_done"], i + 1)
                    chain(V.scalar_tensor_tensor(q_sb[:, i, :], gt[i % 2][:, :], 1.0, q_sb[:, i, :], ALU.add, ALU.mult))
                    V.tensor_tensor(q_sb[:, i, :], q_sb[:, i, :], yb[:, i, :], ALU.add).then_inc(S["y_done"], 1)
                i = s - (AT["ga", 0] + 2)
                if 0 <= i < KT:
                    dve.wait_ge(S["y_hi"], i + 1)
                    dve.wait_ge(S["y_done"], i + 1)
                    V.tensor_tensor(yl[:, i, :], q_sb[:, i, :], yh[:, i, :].bitcast(F32), ALU.subtract)\
                        .then_inc(S["y_lo"], 1)
                if s == 29:
                    dve.wait_ge(S["mod2_ps"], 1)
                    dve.wait_ge(S["y_zero"], 16 * NOVER)
                    V.tensor_copy(mod2c[:, :], bank[7][:, 256:288]).then_inc(S["mod2_sb"], 1)
                if s == 32:
                    dve.wait_ge(S["mod2_T"], 1)
                    V.tensor_copy(mod2r[:, :], psum[0:32, 7, 256:384]).then_inc(S["mod2_row"], 1)

            dve.wait_ge(rows_in, 16 * 5)
            mark(V.tensor_scalar(gate1r[:, :], gate1r[:, :], 0.5, None, ALU.mult))
            chain(V.tensor_scalar(a2r[:, :], a2r[:, :], 1.0, None, ALU.add))
            chain(V.tensor_tensor(zt[:, :], b1r[:, :], a2r[:, :], ALU.mult))
            mark(V.tensor_tensor(a2r[:, :], a2r[:, :], g1r[:, :], ALU.mult))
            chain(V.tensor_tensor(b2r[:, :], b2r[:, :], zt[:, :], ALU.add))
            mark(V.tensor_scalar(g1r[:, :], g1r[:, :], ALPHA, None, ALU.mult))
            chain(V.tensor_scalar(b1r[:, :], b1r[:, :], ALPHA, None, ALU.mult))
            dve.wait_ge(x1_in, 16 * NT)
            for t in range(NT):
                b0 = 2 * (t % 2)
                yv = psum[:, b0:b0 + 2, :].rearrange("p a n -> p (a n)")
                dve.wait_ge(S["wout_ps"], 2 * (t + 1))
                if t >= 1:
                    dve.wait_ge(S["xn_used"], t)
                    dve.wait_ge(S["u2_done"], t)
                V.tensor_tensor(zt[:, :], yv, gate1r[:, :], ALU.mult).then_inc(S["fin_n"], 1)
                dve.wait_ge(S["fin_n"], t + 1)
                chain(V.scalar_tensor_tensor(zt[:, :], x1[:, t, :], ALPHA, zt[:, :], ALU.mult, ALU.add))
                for a in range(2):
                    k_ = mark(V.bn_stats(stats[:, a, :], zt[:, a * 512:(a + 1) * 512]))
                dve.wait_ge(S["dve_order"], k_)
                V.bn_aggr(aggr[:, t, :], stats[:, :, :].rearrange("p a b -> p (a b)")).then_inc(S["ln_sqrt_in"], 1)
                dve.wait_ge(S["ln_sqrt_in"], t + 1)
                dve.wait_ge(S["ln_sqrt"], t + 1)
                chain(V.reciprocal(rstd[:, t:t + 1], rstd[:, t:t + 1]))
                V.tensor_scalar(zt[:, :], zt[:, :], aggr[:, t, 0:1], rstd[:, t:t + 1], ALU.subtract, ALU.mult)\
                    .then_inc(S["xn_done"], 1)
                dve.wait_ge(S["xn_done"], t + 1)
                if t >= 2:
                    dve.wait_ge(S["u2T_ps"], t - 1)
                    dve.wait_ge(u2_st[t % 2], 16 * (t // 2))
                v = u2[t % 2][:, :]
                chain(V.tensor_tensor(v, zt[:, :], a2r[:, :], ALU.mult))
                V.tensor_tensor(v, v, b2r[:, :], ALU.add).then_inc(S["u2_done"], 1)

            dve.wait_ge(S["logits_ps"], NT)
            dve.wait_ge(S["wout_ps"], 2 * NT)
            lgp = bank[6][:, 0:64].rearrange("p (t e) -> p t e", t=NT)
            b3 = [P, NT, NE]
            chain(V.tensor_reduce(red[:, 0, :], lgp, AX.X, ALU.max))
            V.tensor_tensor(lg_[:, :, :], lgp, red[:, 0, :].unsqueeze(2).to_broadcast(b3), ALU.subtract)\
                .then_inc(S["rt_exp_in"], 1)
            mark(V.memset(mpre[:, 0, :], 0.0))
            dve.wait_ge(S["rt_exp"], 1)
            chain(V.tensor_reduce(red[:, 1, :], sc[:, :, :], AX.X, ALU.add))
            chain(V.reciprocal(red[:, 1, :], red[:, 1, :]))
            chain(V.tensor_tensor(sc[:, :, :], sc[:, :, :], red[:, 1, :].unsqueeze(2).to_broadcast(b3), ALU.mult))

            def ranks(out3, in3, n):
                i_of = in3.unsqueeze(3).to_broadcast([P, n, 4, 4])
                j_of = in3.unsqueeze(2).to_broadcast([P, n, 4, 4])
                ge = cge[:, 0:16 * n].rearrange("p (g i j) -> p g i j", i=4, j=4)
                gtr = cgt[:, 0:16 * n].rearrange("p (g i j) -> p g i j", i=4, j=4)
                k_ge = mark(V.tensor_tensor(ge, i_of, j_of, ALU.is_ge))
                k_gt = mark(V.tensor_tensor(gtr, i_of, j_of, ALU.is_gt))
                f1 = cge[:, 0:16 * n].rearrange("p (g m) -> p g m", m=16)
                f2 = cgt[:, 0:16 * n].rearrange("p (g m) -> p g m", m=16)
                dve.wait_ge(S["dve_order"], k_ge)
                mark(V.tensor_tensor(f1, f1, cst[:, C_LT:C_LT + 16].unsqueeze(1).to_broadcast([P, n, 16]), ALU.mult))
                dve.wait_ge(S["dve_order"], k_gt)
                chain(V.tensor_tensor(f2, f2, cst[:, C_GT:C_GT + 16].unsqueeze(1).to_broadcast([P, n, 16]), ALU.mult))
                chain(V.tensor_tensor(cge[:, 0:16 * n], cge[:, 0:16 * n], cgt[:, 0:16 * n], ALU.add))
                chain(V.tensor_reduce(out3, cge[:, 0:16 * n].rearrange("p (g i j) -> p g j i", i=4, j=4), AX.X, ALU.add))

            sc3 = sc[:, :, :].rearrange("p t (g e) -> p (t g) e", g=GRP)
            ranks(rank[:, :, :], sc3, 16)
            chain(V.scalar_tensor_tensor(sel[:, :, :], rank[:, :, :], 2.0, sc3, ALU.is_lt, ALU.mult))
            chain(V.tensor_reduce(gsc[:, :, :].rearrange("p t g -> p (t g)"), sel[:, :, :], AX.X, ALU.add))
            ranks(grank[:, :, :], gsc[:, :, :], 4)
            chain(V.tensor_scalar(grank[:, :, :], grank[:, :, :], 0.0, None, ALU.is_equal))
            gb_ = grank[:, :, :].rearrange("p t g -> p (t g)").unsqueeze(2).to_broadcast([P, 16, 4])
            for r in range(2):
                v = r2[:, r, :, :].rearrange("p t (g e) -> p (t g) e", g=GRP)
                k_ = mark(V.scalar_tensor_tensor(v, rank[:, :, :], float(r), gb_, ALU.is_equal, ALU.mult))
            dve.wait_ge(S["dve_order"], k_)
            chain(V.tensor_tensor(mm[:, :, :], r2[:, 0, :, :], r2[:, 1, :, :], ALU.add))
            chain(V.tensor_copy(mpre[:, 1, :], mm[:, 0, :]))
            chain(V.tensor_tensor(mpre[:, 2, :], mpre[:, 1, :], mm[:, 1, :], ALU.add))
            chain(V.tensor_tensor(mpre[:, 3, :], mpre[:, 2, :], mm[:, 2, :], ALU.add))
            V.tensor_tensor(mtot[:, :], mpre[:, 3, :], mm[:, 3, :], ALU.add).then_inc(S["m_done"], 1)
            two = [P, 2, NT, NE]

            def of_choice(out_, v4):
                chain(V.tensor_tensor(t128[:, :, :, :], r2[:, :, :, :], v4, ALU.mult))
                return mark(V.tensor_reduce(out_, t128[:, :, :, :], AX.X, ALU.add))

            k_ = of_choice(wr[:, :, :], sc[:, :, :].unsqueeze(1).to_broadcast(two))
            dve.wait_ge(S["dve_order"], k_)
            chain(V.tensor_tensor(wsum[:, :], wr[:, 0, :], wr[:, 1, :], ALU.add))
            dve.wait_ge(S["pos_ps"], 1)
            k_pos = mark(V.tensor_copy(pos[:, :, :], bank[7][:, 0:64].rearrange("p (t e) -> p t e", t=NT)))
            k_cnt = mark(V.tensor_copy(cnt[:, :], bank[7][:, 64:80]))
            mark(V.reciprocal(wsum[:, :], wsum[:, :]))
            dve.wait_ge(S["dve_order"], k_cnt)
            k_ovc = mark(V.tensor_scalar(ovc[:, :], cnt[:, :], 129.0, None, ALU.is_ge))
            chain(V.tensor_tensor(t128[:, :, :, :], r2[:, :, :, :], pos[:, :, :].unsqueeze(1).to_broadcast(two), ALU.mult))
            k_ovc = mark(V.scalar_tensor_tensor(ovc[:, :], cnt[:, :], 257.0, ovc[:, :], ALU.is_ge, ALU.add))
            k_pr = mark(V.tensor_reduce(pr[:, :, :], t128[:, :, :, :], AX.X, ALU.add))
            dve.wait_ge(S["dve_order"], k_ovc)
            k_ovc = mark(V.scalar_tensor_tensor(ovc[:, :], cnt[:, :], 385.0, ovc[:, :], ALU.is_ge, ALU.add))
            dve.wait_ge(S["dve_order"], k_pr)
            k_wb = mark(V.tensor_scalar(wb[:, :, :], pr[:, :, :], 128.0, None, ALU.is_ge))
            dve.wait_ge(S["dve_order"], k_ovc)
            k_ovi = mark(V.tensor_tensor_scan(ovi[:, :], ones[:, 0:NE], ovc[:, :], 0.0, ALU.mult, ALU.add))
            dve.wait_ge(S["dve_order"], k_wb)
            k_wb = mark(V.scalar_tensor_tensor(wb[:, :, :], pr[:, :, :], 256.0, wb[:, :, :], ALU.is_ge, ALU.add))
            dve.wait_ge(S["dve_order"], k_ovi)
            k_ovs = mark(V.tensor_tensor(ovs[:, :], ovi[:, :], ovc[:, :], ALU.subtract))
            dve.wait_ge(S["dve_order"], k_wb)
            k_wb = mark(V.scalar_tensor_tensor(wb[:, :, :], pr[:, :, :], 384.0, wb[:, :, :], ALU.is_ge, ALU.add))
            dve.wait_ge(S["dve_order"], k_ovs)
            ebc = cst[:, C_EXP:C_EXP + NE]
            first = ctrlf[:, FIRST:FIRST + NE]
            k_first = mark(V.tensor_tensor(first, ovs[:, :], ebc, ALU.add))
            dve.wait_ge(S["dve_order"], k_wb)
            k_pr = mark(V.scalar_tensor_tensor(pr[:, :, :], wb[:, :, :], -128.0, pr[:, :, :], ALU.mult, ALU.add))
            dve.wait_ge(S["dve_order"], k_first)
            k_fr = of_choice(fr[:, :, :], first.unsqueeze(1).unsqueeze(1).to_broadcast(two))
            dve.wait_ge(iota_in, 16)
            dve.wait_ge(S["dve_order"], k_fr)
            chain(V.tensor_tensor(fr[:, :, :], fr[:, :, :], wb[:, :, :], ALU.add))
            for t in range(NT):
                for r in range(2):
                    mark(V.tensor_scalar(at_pos[:, r, t, :], iota[:, :], pr[:, r, t:t + 1], None, ALU.is_equal))
                    V.tensor_scalar(at_blk[:, r, t, :], iota[:, 0:TCOL], fr[:, r, t:t + 1], cst[:, C_TOK + t:C_TOK + t + 1],
                                    ALU.is_equal, ALU.mult).then_inc(S["onehots"], 1)
            mark(V.tensor_tensor(wA[:, :], wr[:, 0, :], wsum[:, :], ALU.mult))
            mark(V.tensor_tensor(wB[:, :], wr[:, 1, :], wsum[:, :], ALU.mult))
            mark(V.tensor_copy(ctrlf[:, MORE:MORE + NE], ovc[:, :]))
            mark(V.tensor_tensor(ctrlf[:, LAST:LAST + NE], ovi[:, :], ebc, ALU.add))
            chain(V.tensor_scalar(ctrlf[:, NUM:NUM + 1], ovi[:, NE - 1:NE], float(NE), None, ALU.add))
            V.tensor_copy(ctrl[:, :], ctrlf[:, :]).then_inc(S["ctrl_done"], 1)
            dve.wait_ge(S["idx_ps"], 1)
            V.tensor_copy(idx[:, :], bank[7][:, 128:128 + TCOL]).then_inc(S["idx_ready"], 1)
            chain(V.tensor_scalar(yrf[:, :, :], fr[:, :, :], 1.0, float(P), ALU.add, ALU.mult))
            chain(V.tensor_tensor(yrf[:, :, :], yrf[:, :, :], pr[:, :, :], ALU.add))
            chain(V.tensor_copy(yrow[:, :, :], yrf[:, :, :]))

            def lo(b, par, ch):
                dve.wait_ge(S["mhi_done"], b * CH + (ch + 1))
                V.tensor_tensor(mlo[ch % HLR][:, :, :], mraw[par][ch][:, :].rearrange("p (k f) -> p k f", k=2),
                                mhi[ch % HLR][:, :, :].bitcast(F32), ALU.subtract).then_inc(S["mlo_done"], 1)

            def lo_half(b, par, a):
                dve.wait_ge(S["mhi_done"], b * CH + CH)
                return V.tensor_tensor(mlo[(CH - 1) % HLR][:, a, :], mraw[par][CH - 1][:, a * 512:(a + 1) * 512],
                                       mhi[(CH - 1) % HLR][:, a, :].bitcast(F32), ALU.subtract)

            def x_lo(b):
                for a in range(2):
                    dve.wait_ge(S["xTh_m"], b * 2 + (a + 1))
                    V.tensor_tensor(xTl[:, 4 * a:4 * a + 4, :], psum[:, 2 + a, :].rearrange("p (k n) -> p k n", k=4),
                                    xTh[:, 4 * a:4 * a + 4, :].bitcast(F32), ALU.subtract).then_inc(S["xTl_m"], 1)

            def dve_block(b, par):
                for ch in range(CH - 1):
                    lo(b, par, ch)
                dve.wait_ge(S["chunk_used"], b * CH + (HLR + 8))
                dve.wait_ge(S["silu_done"], b + 1)
                for a in range(2):
                    v = h_sb[:, 256 * a:256 * a + 256]
                    V.tensor_tensor(v, v, bank[1][:, 256 * a:256 * a + 256], ALU.mult).then_inc(S["h_done_m"], 1)
                lo_half(b, par, 0)
                for a in range(2):
                    dve.wait_ge(S["hTh_done"], b * 2 + (a + 1))
                    V.tensor_tensor(hTl[:, 2 * a:2 * a + 2, :],
                                    bank[4 + 3 * a][:, 0:256].rearrange("p (k n) -> p k n", k=2),
                                    hTh[:, 2 * a:2 * a + 2, :].bitcast(F32), ALU.subtract).then_inc(S["hTl_done"], 1)
                lo_half(b, par, 1).then_inc(S["mlo_done"], 1)
                x_lo(b + 1)

            x_lo(0)
            with dve.Fori(0, NE // 2) as pair:
                for par in range(2):
                    first = dve.value_load(ctrl[0:1, bass.ds(2 * pair + (FIRST + par), 1)], min_val=0, max_val=NBLK - 1)
                    more = dve.value_load(ctrl[0:1, bass.ds(2 * pair + (MORE + par), 1)], min_val=0, max_val=3)
                    dve_block(first, par)
                    with dve.If(more > 0):
                        with dve.Fori(0, more) as j:
                            dve_block(first + 1 + j, par)

            dve.wait_ge(rows_in, 16 * 8)
            dve.wait_ge(S["x1_done"], NT)
            def residual(t):
                z, ya_, yb_ = fin[t]
                dve.wait_ge(S["fin_a"], t + 1)
                chain(V.scalar_tensor_tensor(z[:, :], yb_[:, :], wB[:, t:t + 1], ya_[:, :], ALU.mult, ALU.add))
                chain(V.tensor_tensor(z[:, :], z[:, :], gate2r[:, :], ALU.mult))
                V.tensor_tensor(z[:, :], z[:, :], x1[:, t, :], ALU.add).then_inc(S["fin_z"], 1)

            def normalise(t):
                z, ya_, yb_ = fin[t]
                dve.wait_ge(S["fin_sqrt"], t + 1)
                chain(V.reciprocal(rstd[:, t:t + 1], rstd[:, t:t + 1]))
                chain(V.scalar_tensor_tensor(z[:, :], z[:, :], fsum[:, t, 1:2], g2r[:, :], ALU.add, ALU.mult))
                V.scalar_tensor_tensor(z[:, :], z[:, :], rstd[:, t:t + 1], be2r[:, :], ALU.mult, ALU.add)\
                    .then_inc(S["fin_out"], 1)

            residual(0)
            for t in range(NT):
                if t + 1 < NT:
                    residual(t + 1)
                normalise(t)

        @block.tensor
        def _(pe):
            mmul = nc.tensor.matmul
            pe.sem_inc(S["chunk_used"], HLR)
            pe.wait_ge(const_in, 16)
            pe.wait_ge(param_in, 16 * 5)
            nc.tensor.transpose(bank[7][:, 0:64], prm[:, :], ident[0:64, 0:64]).then_inc(S["pcol_ps"], 1)
            pe.wait_ge(S["setup_done"], 4)
            pe.wait_ge(S["pool_in"], 16 * 5)
            mmul(psum[0:NQ, 6, 0:384], rbs[:, :], cst[0:NBUCKET + 1, C_HOT:C_HOT + 384], start=True, stop=True)\
                .then_inc(S["bvec_ps"], 1)
            pe.wait_ge(small_in, 32)
            pe.wait_ge(S["ada1_sum"], 6)
            for _ in range(4):
                mmul(bank[0], ident, cst[:, 0:512], start=True, stop=True)
            pe.wait_ge(S["ada1_sum"], 8)
            for n in range(16):
                mmul(bank[4][:, n:n + 1], ada1[:, 0, n * P:(n + 1) * P], ones[:, 0:1],
                     start=(n == 0), stop=False, skip_group_check=True)
            mmul(bank[4][:, 0:16], adab1[:, :], ident[0:16, 0:16], start=False, stop=True,
                 skip_group_check=True).then_inc(S["mod1_ps"], 1)
            pe.wait_ge(x_in, 16 * NT)
            for k in range(KT):
                if k >= 4:
                    pe.wait_ge(S["u_hi"], k - 3)
                    pe.wait_ge(S["u_even"], (k - 4) // 2 + 1)
                    if k % 2 == 1:
                        pe.wait_ge(S["u_odd"], (k - 4) // 2 + 1)
                for t in range(NT):
                    ins = nc.tensor.transpose(bank[XB[k % 4]][:, t * P:(t + 1) * P], x_sb[:, t, k * P:(k + 1) * P], ident)
                ins.then_inc(S["xT_ps"], 1)

            def project(s):
                h, l = whi[s % 3], wlo[s % 3]
                pe.wait_ge(S["split_lo"], s + 1)
                if s >= 2:
                    pe.wait_ge(S["evac"], s - 1)
                elif s == 1:
                    pe.wait_ge(S["u_lo"], KT)
                for k in range(KT):
                    if s == 0:
                        pe.wait_ge(S["u_lo"], k + 1)
                    mmul(bank[s % 2], h[:, k, :], uh[:, k, :], start=(k == 0), stop=False)
                    mmul(bank[s % 2], h[:, k, :], ul[:, k, :], start=False, stop=False)
                    ins = mmul(bank[s % 2], l[:, k, :], uh[:, k, :], start=False, stop=(k == KT - 1))
                ins.then_inc(S["proj_ps"], 1)

            for s in range(NPROJ):
                project(s)
                if s == 3:
                    pe.wait_ge(S["evac"], 2)
                    for t in range(NT):
                        ins = nc.tensor.transpose(bank[5][:, t * P:(t + 1) * P], tt[0][:, t * P:(t + 1) * P], ident)
                    ins.then_inc(S["v_ps"], 1)
                n = UNIT_AT.get(s - 4)
                if n is not None:
                    pe.wait_ge(S["on_done"], n + 1)
                    if n >= 1:
                        pe.wait_ge(S["ya_done"], n)
                    if s == 29:
                        pe.wait_ge(S["mod2_sb"], 1)
                    if s == 32:
                        pe.wait_ge(S["mod2_row"], 1)
                    for a in range(2):
                        ins = nc.tensor.transpose(bank[7][:, a * P:(a + 1) * P], onrm[:, a * P:(a + 1) * P], ident)
                    ins.then_inc(S["ot_ps"], 1)
                n = UNIT_AT.get(s - 3)
                if n is not None:
                    blk_, kv = n % 4, n // 8
                    pe.wait_ge(S["pt_sb"], n + 1)
                    pe.wait_ge(S["v_sb"], 1)
                    if n >= 1:
                        pe.wait_ge(S["on_done"], n)
                    for a in range(2):
                        for b in range(2):
                            hh = 2 * b + a
                            halves = [1] if blk_ == 0 else [0, 1]
                            for half in halves:
                                ins = mmul(bank[6][:, hh * HD:(hh + 1) * HD], ptb[:, a, b, half, :],
                                           vv[:, blk_ - 1 + half, kv * HD:(kv + 1) * HD],
                                           start=(half == halves[0]), stop=(half == 1))
                    ins.then_inc(S["o_ps"], 1)
                n = UNIT_AT.get(s - 2)
                if n is not None:
                    pe.wait_ge(S["exp_done"], 5 * (n + 1))
                    if n >= 1:
                        pe.wait_ge(S["pt_sb"], n)
                    for a in range(2):
                        for b in range(2):
                            for half in ([1] if n % 4 == 0 else [0, 1]):
                                ins = nc.tensor.transpose(ptps[:, a, b, half, :],
                                                          ssb[n % 2][:, a, b, half * P:(half + 1) * P], ident)
                    ins.then_inc(S["pt_ps"], 1)
                n = UNIT_AT.get(s)
                if n is not None:
                    hg, blk_ = n // 4, n % 4
                    lo_ = P if blk_ == 0 else 0
                    pe.wait_ge(S["evac"], AT["q", 2 * hg + 1] + 1)
                    pe.wait_ge(kdup_in, 32)
                    if n >= 1:
                        pe.wait_ge(S["logit_done"], n)
                    for b in range(2):
                        for a in range(2):
                            rows_ = slice(64 * a, 64 * a + 64)
                            ins = mmul(scores[:, a, b, lo_:256], q_sb[rows_, 2 * hg + b, blk_ * P:(blk_ + 1) * P],
                                       kk[hg // 2][rows_, blk_ * P - P + lo_:(blk_ + 1) * P], start=True, stop=True)
                    ins.then_inc(S["sc_ps"], 1)
                i = s - 4
                if 0 <= i < KT:
                    pe.wait_ge(S["conv_done"], i + 1)
                    pe.wait_ge(lruw_in, 32)
                    if i >= 1:
                        pe.wait_ge(S["er_done"], i)
                        pe.wait_ge(S["ti_done"], i)
                    mmul(bank[6], wax[:, 0, i, :], xc[i % 2][:, :], start=True, stop=True).then_inc(S["lr_ps"], 1)
                    mmul(bank[7], wax[:, 1, i, :], xc[i % 2][:, :], start=True, stop=True).then_inc(S["li_ps"], 1)
                if s == 28:
                    pe.wait_ge(S["ada2_used"], 16)
                    pe.wait_ge(S["ya_done"], max(n for n in range(NU) if START[n] + 4 <= s) + 1)
                    for n in range(32):
                        ins = mmul(bank[7][:, 256 + n:257 + n], acc2[:, n * P:(n + 1) * P], ones[:, 0:1],
                                   start=(n == 0), stop=False, skip_group_check=True)
                    mmul(bank[7][:, 256:288], adab2[:, :], ident[0:32, 0:32], start=False, stop=True,
                         skip_group_check=True).then_inc(S["mod2_ps"], 1)
                if s == 31:
                    pe.wait_ge(S["mod2_sb"], 1)
                    pe.wait_ge(S["ya_done"], max(n for n in range(NU) if START[n] + 4 <= s) + 1)
                    nc.tensor.transpose(psum[0:32, 7, 256:384], mod2c[:, :], ident).then_inc(S["mod2_T"], 1)

            def to_router(t):
                pe.wait_ge(S["u2_done"], t + 1)
                if t == 1:
                    pe.wait_ge(S["fin_n"], 3)
                if t >= 2:
                    pe.wait_ge(S["u2T_sb"], t - 1)
                for k in range(KT):
                    ins = nc.tensor.transpose(psum[:, 4 * (1 - t % 2) + k // 4, (k % 4) * P:(k % 4 + 1) * P],
                                              u2[t % 2][:, k * P:(k + 1) * P], ident)
                ins.then_inc(S["u2T_ps"], 1)

            def logits(t):
                pe.wait_ge(S["u2T_sb"], t + 1)
                o_ = bank[6][:, t * NE:(t + 1) * NE]
                mmul(o_, ones[0:1, :], rbr[:, :], start=True, stop=False)
                for k in range(KT):
                    ins = mmul(o_, u2T[t % 2][:, k, :], rw[:, k, :], start=False, stop=(k == KT - 1))
                ins.then_inc(S["logits_ps"], 1)

            def out_product(t, n, k):
                o_ = bank[2 * (t % 2) + n]
                a, b = yh[:, k, t * P:(t + 1) * P], yl[:, k, t * P:(t + 1) * P]
                cols = slice(n * 512, (n + 1) * 512)
                mmul(o_, a, woh[k][:, cols], start=(k == 0), stop=False)
                mmul(o_, a, wol[k][:, cols], start=False, stop=False)
                return mmul(o_, b, woh[k][:, cols], start=False, stop=(k == KT - 1))

            for k in range(KT):
                pe.wait_ge(S["y_lo"], k + 1)
                pe.wait_ge(S["split_lo"], NPROJ + k + 1)
                if k == 0:
                    pe.wait_ge(S["evac"], NPROJ)
                    pe.wait_ge(S["logit_done"], NU)
                for t in range(2):
                    if k < KT - 2:
                        for n in range(2):
                            out_product(t, n, k)
            for t in range(2):
                for k in range(KT - 2, KT):
                    for n in range(2):
                        ins = out_product(t, n, k)
                ins.then_inc(S["wout_ps"], 2)
            for t in range(2, NT):
                for n in range(2):
                    pe.wait_ge(S["fin_n"], t - 1)
                    for k in range(KT):
                        ins = out_product(t, n, k)
                    ins.then_inc(S["wout_ps"], 1)
                    if t == 3 and n == 0:
                        to_router(0)
            to_router(1)
            logits(0)
            to_router(2)
            logits(1)
            logits(2)
            to_router(NT - 1)
            logits(NT - 1)
            pe.wait_ge(S["m_done"], 1)
            f = bank[7][:, 0:64]
            mmul(f, cst[:, C_LOW:C_LOW + P], mm[:, :, :].rearrange("p t e -> p (t e)"), start=True, stop=False)
            mmul(f, ones[:, :], mpre[:, :, :].rearrange("p t e -> p (t e)"), start=False, stop=True)
            mmul(bank[7][:, 64:80], ones[:, :], mtot[:, :], start=True, stop=True, skip_group_check=True)\
                .then_inc(S["pos_ps"], 1)
            for t in range(NT):
                for r in range(2):
                    pe.wait_ge(S["onehots"], 2 * t + r + 1)
                    ins = mmul(bank[7][:, 128:128 + TCOL], at_pos[:, r, t, :], at_blk[:, r, t, :],
                               start=(t == 0 and r == 0), stop=(t == NT - 1 and r == 1), skip_group_check=True)
            ins.then_inc(S["idx_ps"], 1)
            for a in range(2):
                mmul(bank[5 + a], ones[0:1, :], x1[0:1, 0, a * 512:(a + 1) * 512], start=True, stop=True)

            def xpose(b, a):
                for k in range(4 * a, 4 * a + 4):
                    ins = nc.tensor.transpose(psum[:, 2 + a, (k % 4) * P:(k % 4 + 1) * P],
                                              xg_m[:, k * P:(k + 1) * P], ident)
                return ins

            def chunk(b, ch):
                pe.wait_ge(S["mlo_done"], b * CH + (ch + 1))
                h, l = mhi[ch % HLR], mlo[ch % HLR]
                if ch < 8:
                    o_ = bank[ch // 4]
                    for i in range(2):
                        k = 2 * (ch % 4) + i
                        first, last = ch % 4 == 0 and i == 0, ch % 4 == 3 and i == 1
                        mmul(o_, xTh[:, k, :], h[:, i, :], start=first, stop=False)
                        mmul(o_, xTh[:, k, :], l[:, i, :], start=False, stop=False)
                        ins = mmul(o_, xTl[:, k, :], h[:, i, :], start=False, stop=last)
                else:
                    k = ch - 8
                    for i in range(2):
                        mmul(bank[5 + i], hTh[:, k, :], h[:, i, :], start=(k == 0), stop=False)
                        mmul(bank[5 + i], hTh[:, k, :], l[:, i, :], start=False, stop=False)
                    for i in range(2):
                        ins = mmul(bank[5 + i], hTl[:, k, :], h[:, i, :], start=False, stop=(k == FT - 1))
                ins.then_inc(S["chunk_used"], 1)

            def pe_block(b):
                pe.wait_ge(S["xTl_m"], b * 2 + 2)
                pe.wait_ge(S["h_done_m"], b * 2 + 2)
                for ch in range(8):
                    chunk(b, ch)
                pe.wait_ge(S["gath"], b * 16 + 32)
                xpose(b + 1, 0)
                for a in range(2):
                    pe.wait_ge(S["h_done_m"], b * 2 + (a + 3))
                    for k in range(2 * a, 2 * a + 2):
                        ins = nc.tensor.transpose(bank[4 + 3 * a][:, (k % 2) * P:(k % 2 + 1) * P], h_sb[:, k * P:(k + 1) * P], ident)
                    ins.then_inc(S["hT_ps"], 1)
                xpose(b + 1, 1).then_inc(S["xT_m_ps"], 1)
                pe.wait_ge(S["y_ev"], b * 2 + 2)
                for ch in range(8, CH):
                    if ch % 2 == 0:
                        pe.wait_ge(S["hTl_done"], b * 2 + (ch // 2 - 3))
                    chunk(b, ch)

            pe.wait_ge(S["gath"], 16)
            xpose(0, 0)
            xpose(0, 1).then_inc(S["xT_m_ps"], 1)
            pe.wait_ge(S["ctrl_done"], 1)
            nblk = pe.value_load(ctrl[0:1, NUM:NUM + 1], min_val=NE, max_val=NBLK)
            with pe.Fori(0, nblk) as b:
                pe_block(b)


_INS = ["x", "c", "ada_w", "ada_b", "w_in", "attn_sink", "rel_bias", "conv_w", "conv_b", "lru_wa", "lru_ba",
        "lru_wx", "lru_bx", "lru_lambda", "w_out", "ln1_g", "ln1_b", "router_w", "router_b", "moe_w_gate",
        "moe_w_up", "moe_w_down", "ln2_g", "ln2_b"]


def kernel(**inputs):
    import concourse.bacc as _bacc
    from concourse.bass_utils import run_bass_kernel_spmd as _run

    nc = _bacc.Bacc("TRN2", target_bir_lowering=False, num_devices=1)
    arrays, args = {}, []
    for name in _INS + ["consts"]:
        a = constants() if name == "consts" else np.ascontiguousarray(inputs[name])
        arrays[f"in_{name}_dram"] = a
        args.append(nc.dram_tensor(f"in_{name}_dram", a.shape, mybir.dt.from_np(a.dtype), kind="ExternalInput").ap())
    out = nc.dram_tensor("out_0_dram", (1, T, D), F32, kind="ExternalOutput").ap()
    hybrid_layer(nc, *args, out)
    r = _run(nc, [arrays], core_ids=[0])
    return r.results[0]["out_0_dram"]
```
